# Optimizing a Trainium2 kernel written in Bass

```python
import jax, jax.numpy as jnp
from jax import lax
import numpy as np

D_MODEL = 1024
BATCH = 1
SEQ = 256
DEPTH = 2

CHUNK = 128
A_GROUPS = 8
A_WIDTH = 1024
A_GROUP_DIM = A_WIDTH // A_GROUPS
POOL_WINDOWS = (2, 4, 8, 16)
B_GROUPS = len(POOL_WINDOWS)
B_GROUP_DIM = 128
B_WIDTH = B_GROUPS * B_GROUP_DIM
C_WIDTH = 512
CONV_WIDTH = 3
D_HEADS = 8
HEAD_DIM = 64
D_WIDTH = D_HEADS * HEAD_DIM
ROT_DIM = HEAD_DIM // 4
ROPE_THETA = 500000.0
MOBA_BLOCK = 256
MOBA_TOPK = 3
MOBA_Q_CHUNK = 64
D_FF = 2816
N_EVEN = (DEPTH + 1) // 2
N_ODD = DEPTH // 2
EPS = 1e-6

kernel_name = "hybrid_gmlp_pool_shortconv_moba_block"

def rms_norm(x, g):
    xf = x.astype(jnp.float32)
    y = xf * lax.rsqrt(jnp.mean(xf * xf, axis=-1, keepdims=True) + EPS)
    return (y * g.astype(jnp.float32)).astype(x.dtype)

def layer_norm(x, g, b):
    xf = x.astype(jnp.float32)
    mu = jnp.mean(xf, axis=-1, keepdims=True)
    var = jnp.mean(jnp.square(xf - mu), axis=-1, keepdims=True)
    y = (xf - mu) * lax.rsqrt(var + EPS)
    return (y * g.astype(jnp.float32) + b.astype(jnp.float32)).astype(x.dtype)

def causal_dwconv(x, w):
    k = w.shape[0]
    return lax.conv_general_dilated(
        x, w[:, None, :].astype(x.dtype), window_strides=(1,), padding=[(k - 1, 0)],
        dimension_numbers=('NWC', 'WIO', 'NWC'), feature_group_count=x.shape[-1])

def spatial_gating(u, v, v_g, v_b, w_s, b_s):
    bsz, s, _ = v.shape
    v = layer_norm(v, v_g, v_b)
    vc = v.reshape(bsz, s // CHUNK, CHUNK, A_GROUPS, A_GROUP_DIM)
    causal = jnp.tril(jnp.ones((CHUNK, CHUNK), dtype=bool))
    w = jnp.where(causal, w_s, jnp.zeros((), w_s.dtype))
    mixed = jnp.einsum('gij,bnjgd->bnigd', w, vc) + b_s.T[None, None, :, :, None]
    return u * mixed.reshape(bsz, s, A_WIDTH)

def multiscale_pool(xb, pool_w, pool_scale):
    bsz, s, _ = xb.shape
    xf = xb.astype(jnp.float32).reshape(bsz, s, B_GROUPS, B_GROUP_DIM)
    cs = jnp.cumsum(xf, axis=1)
    t = jnp.arange(s)
    outs = []
    for gi, w in enumerate(POOL_WINDOWS):
        csg = cs[:, :, gi]
        lag = jnp.pad(csg[:, :s - w], ((0, 0), (w, 0), (0, 0)))
        cnt = jnp.minimum(t + 1, w).astype(jnp.float32)[None, :, None]
        outs.append((csg - lag) / cnt - xf[:, :, gi])
    pooled = jnp.stack(outs, axis=2).astype(xb.dtype)
    mixed = jnp.einsum('bsgd,gde->bsge', pooled, pool_w).reshape(bsz, s, B_WIDTH)
    return mixed * pool_scale

def partial_rotary(x, pos):
    half = ROT_DIM // 2
    inv_freq = ROPE_THETA ** (-jnp.arange(0, ROT_DIM, 2, dtype=jnp.float32) / ROT_DIM)
    ang = pos.astype(jnp.float32)[:, None, :, None] * inv_freq
    cos, sin = jnp.cos(ang), jnp.sin(ang)
    xr = x[..., :ROT_DIM].astype(jnp.float32)
    x1, x2 = xr[..., :half], xr[..., half:]
    rot = jnp.concatenate([x1 * cos - x2 * sin, x2 * cos + x1 * sin], axis=-1)
    return jnp.concatenate([rot.astype(x.dtype), x[..., ROT_DIM:]], axis=-1)

def moba_attention(q, k, v):
    bsz, nh, s, dh = q.shape
    nb = -(-s // MOBA_BLOCK)
    pad = nb * MOBA_BLOCK - s
    kp = jnp.pad(k, ((0, 0), (0, 0), (0, pad), (0, 0)))
    vp = jnp.pad(v, ((0, 0), (0, 0), (0, pad), (0, 0)))
    k_blocks = kp.reshape(bsz, nh, nb, MOBA_BLOCK, dh)
    v_blocks = vp.reshape(bsz, nh, nb, MOBA_BLOCK, dh)
    k_mean = jnp.mean(k_blocks.astype(jnp.float32), axis=3)
    topk = min(MOBA_TOPK, nb)
    scale = dh ** -0.5
    bi = jnp.arange(bsz)[:, None, None, None]
    hi = jnp.arange(nh)[None, :, None, None]

    def chunk(start):
        cur = start // MOBA_BLOCK
        qf = lax.dynamic_slice_in_dim(q, start, MOBA_Q_CHUNK, axis=2).astype(jnp.float32)
        gate = jnp.einsum('bhqd,bhnd->bhqn', qf, k_mean)
        gate = jnp.where(jnp.arange(nb) < cur, gate, -jnp.inf)
        _, idx = lax.top_k(gate, topk)
        valid = jnp.arange(topk) < cur
        k_sel = k_blocks[bi, hi, idx].astype(jnp.float32)
        v_sel = v_blocks[bi, hi, idx].astype(jnp.float32)
        s_sel = jnp.einsum('bhqd,bhqnld->bhqnl', qf, k_sel) * scale
        s_sel = jnp.where(valid[:, None], s_sel, -jnp.inf)
        k_own = lax.dynamic_slice_in_dim(kp, cur * MOBA_BLOCK, MOBA_BLOCK, axis=2).astype(jnp.float32)
        v_own = lax.dynamic_slice_in_dim(vp, cur * MOBA_BLOCK, MOBA_BLOCK, axis=2).astype(jnp.float32)
        s_own = jnp.einsum('bhqd,bhld->bhql', qf, k_own) * scale
        q_pos = start + jnp.arange(MOBA_Q_CHUNK)
        k_pos = cur * MOBA_BLOCK + jnp.arange(MOBA_BLOCK)
        s_own = jnp.where(k_pos[None, :] <= q_pos[:, None], s_own, -jnp.inf)
        logits = jnp.concatenate(
            [s_sel.reshape(bsz, nh, MOBA_Q_CHUNK, topk * MOBA_BLOCK), s_own], axis=-1)
        p = jax.nn.softmax(logits, axis=-1)
        p_sel = p[..., :topk * MOBA_BLOCK].reshape(bsz, nh, MOBA_Q_CHUNK, topk, MOBA_BLOCK)
        p_own = p[..., topk * MOBA_BLOCK:]
        o = (jnp.einsum('bhqnl,bhqnld->bhqd', p_sel, v_sel)
             + jnp.einsum('bhql,bhld->bhqd', p_own, v_own))
        return o.astype(q.dtype)

    starts = jnp.arange(s // MOBA_Q_CHUNK) * MOBA_Q_CHUNK
    out = lax.map(chunk, starts)
    return out.transpose(1, 2, 0, 3, 4).reshape(bsz, nh, s, dh)

def mixer_ab(h, w_in, v_g, v_b, w_s, b_s, pool_w, pool_scale, w_out):
    proj = h @ w_in
    u, v, xb = jnp.split(proj, [A_WIDTH, 2 * A_WIDTH], axis=-1)
    ya = spatial_gating(jax.nn.gelu(u), jax.nn.gelu(v), v_g, v_b, w_s, b_s)
    yb = multiscale_pool(xb, pool_w, pool_scale)
    return jnp.concatenate([ya, yb], axis=-1) @ w_out

def mixer_cd(h, pos, w_in, conv_w, w_out):
    bsz, s, _ = h.shape
    proj = h @ w_in
    cb, cc, cx, q, k, v = jnp.split(
        proj, [C_WIDTH, 2 * C_WIDTH, 3 * C_WIDTH, 3 * C_WIDTH + D_WIDTH, 3 * C_WIDTH + 2 * D_WIDTH], axis=-1)
    yc = cb * causal_dwconv(cc * cx, conv_w)

    def heads(t):
        return t.reshape(bsz, s, D_HEADS, HEAD_DIM).transpose(0, 2, 1, 3)

    qh = partial_rotary(heads(q), pos)
    kh = partial_rotary(heads(k), pos)
    yd = moba_attention(qh, kh, heads(v)).transpose(0, 2, 1, 3).reshape(bsz, s, D_WIDTH)
    return jnp.concatenate([yc, yd], axis=-1) @ w_out

def conv_ffn(h, w_up, conv_w, w_down):
    up = causal_dwconv(h @ w_up, conv_w)
    g, u = jnp.split(up, 2, axis=-1)
    return (jax.nn.silu(g) * u) @ w_down

def setup_inputs(seed: int = 0) -> dict:
    key = jax.random.key(seed)
    ks = jax.random.split(key, 24)
    f32 = jnp.float32

    def dense(k, shape, fan_in):
        return jax.random.normal(k, shape, f32) * (fan_in ** -0.5)

    def gain(k, shape):
        return 1.0 + 0.1 * jax.random.normal(k, shape, f32)

    x = jax.random.normal(ks[0], (BATCH, SEQ, D_MODEL), f32)
    c = jax.random.normal(ks[1], (BATCH, D_MODEL), f32)
    offset = jax.random.randint(ks[2], (BATCH,), 0, 2048, dtype=jnp.int32)
    positions = offset[:, None] + jnp.arange(SEQ, dtype=jnp.int32)[None, :]
    return {
        'x': x,
        'c': c,
        'positions': positions,
        'ab_w_in': dense(ks[3], (N_EVEN, D_MODEL, 2 * A_WIDTH + B_WIDTH), D_MODEL),
        'ab_vnorm_g': gain(ks[4], (N_EVEN, A_WIDTH)),
        'ab_vnorm_b': 0.1 * jax.random.normal(ks[5], (N_EVEN, A_WIDTH), f32),
        'ab_spatial_w': dense(ks[6], (N_EVEN, A_GROUPS, CHUNK, CHUNK), CHUNK),
        'ab_spatial_b': gain(ks[7], (N_EVEN, A_GROUPS, CHUNK)),
        'ab_pool_w': dense(ks[8], (N_EVEN, B_GROUPS, B_GROUP_DIM, B_GROUP_DIM), B_GROUP_DIM),
        'ab_pool_scale': gain(ks[9], (N_EVEN, B_WIDTH)),
        'ab_w_out': dense(ks[10], (N_EVEN, A_WIDTH + B_WIDTH, D_MODEL), A_WIDTH + B_WIDTH),
        'cd_w_in': dense(ks[11], (N_ODD, D_MODEL, 3 * C_WIDTH + 3 * D_WIDTH), D_MODEL),
        'cd_conv_w': dense(ks[12], (N_ODD, CONV_WIDTH, C_WIDTH), CONV_WIDTH),
        'cd_w_out': dense(ks[13], (N_ODD, C_WIDTH + D_WIDTH, D_MODEL), C_WIDTH + D_WIDTH),
        'ffn_w_up': dense(ks[14], (DEPTH, D_MODEL, 2 * D_FF), D_MODEL),
        'ffn_conv_w': dense(ks[15], (DEPTH, CONV_WIDTH, 2 * D_FF), CONV_WIDTH),
        'ffn_w_down': dense(ks[16], (DEPTH, D_FF, D_MODEL), D_FF),
        'ada_w': 0.02 * jax.random.normal(ks[17], (DEPTH, D_MODEL, 6 * D_MODEL), f32),
        'ada_b': 0.02 * jax.random.normal(ks[18], (DEPTH, 6 * D_MODEL), f32),
        'norm_g': gain(ks[19], (DEPTH, 4, D_MODEL)),
    }

def reference(x, c, positions, ab_w_in, ab_vnorm_g, ab_vnorm_b, ab_spatial_w, ab_spatial_b,
              ab_pool_w, ab_pool_scale, ab_w_out, cd_w_in, cd_conv_w, cd_w_out,
              ffn_w_up, ffn_conv_w, ffn_w_down, ada_w, ada_b, norm_g):
    c_act = jax.nn.silu(c)
    for i in range(DEPTH):
        mod = (c_act @ ada_w[i] + ada_b[i])[:, None, :]
        sh1, sc1, gt1, sh2, sc2, gt2 = jnp.split(mod, 6, axis=-1)
        g = norm_g[i]
        h = rms_norm(x, g[0]) * (1.0 + sc1) + sh1
        j = i // 2
        if i % 2 == 0:
            y = mixer_ab(h, ab_w_in[j], ab_vnorm_g[j], ab_vnorm_b[j], ab_spatial_w[j],
                         ab_spatial_b[j], ab_pool_w[j], ab_pool_scale[j], ab_w_out[j])
        else:
            y = mixer_cd(h, positions, cd_w_in[j], cd_conv_w[j], cd_w_out[j])
        x = x + gt1 * rms_norm(y, g[1])
        h = rms_norm(x, g[2]) * (1.0 + sc2) + sh2
        y = conv_ffn(h, ffn_w_up[i], ffn_conv_w[i], ffn_w_down[i])
        x = x + gt2 * rms_norm(y, g[3])
    return x


_drawn_inputs = setup_inputs


def setup_inputs(seed=0):
    import zlib

    import numpy as np

    out = dict(_drawn_inputs(seed))
    spreads = {}
    factors = {}
    for name, (base, spread) in spreads.items():
        noise = np.random.default_rng([zlib.crc32(name.encode()), seed]).standard_normal(out[name].shape)
        drawn = base * np.exp(spread * noise) if base else spread * noise
        out[name] = __import__('jax').numpy.asarray(drawn.astype(out[name].dtype))
    for name, factor in factors.items():
        out[name] = (out[name] * factor).astype(out[name].dtype)
    return out
```

```python
from contextlib import ExitStack

import numpy as np

import concourse.bass as bass
from concourse import mybir

F32 = mybir.dt.float32
F32R = mybir.dt.float32r
BF16 = mybir.dt.bfloat16
I32 = mybir.dt.int32
ALU = mybir.AluOpType
ACT = mybir.ActivationFunctionType
AX_X = mybir.AxisListType.X

P = 128
TOK = 256
NT = TOK // P
D = 1024
KD = D // P
A_GROUPS = 8
A_WIDTH = 1024
WINDOWS = (2, 4, 8, 16)
NB = len(WINDOWS)
PAD = max(WINDOWS)
C_WIDTH = 512
HEADS = 8
HD = 64
ROT = HD // 4
HALF = ROT // 2
FF = 2816
FCH = FF // P
STEPS = FCH // 2
EPS = 1e-6
BIG = 1e30

TILE = 2048
RAW = 6
RING = 3
LO_DVE = 768
PRO = 8
AB0, FF0, CD0, FF1, END = 0, 16, 49, 65, 98

R_NORM, R_POOL, R_CONV, R_ALL = 0, 64, 68, 80

LOOP_K = 5
REST = range(LOOP_K, KD)
ADA_TILES = [(v, k) for v in (2, 3, 4, 5) for k in range(KD)] + [(v, k) for v in (6, 7) for k in REST]
ADA_AB = {3: 2, 4: 2, 5: 2, 6: 2, 7: 2, 8: 2, 9: 2, 10: 2, 11: 2, 12: 2, 13: 2, 14: 2, 15: 3, 16: 3, 17: 2}
LATE0 = 6
ADA_FF = len(ADA_TILES)
LOOP_V = (6, 7, 9, 10)
ADA_TILES += [(v, k) for k in range(LOOP_K) for v in LOOP_V]
ADA_MID = len(ADA_TILES)
ADA_TILES += [(v, k) for v in (9, 10) for k in REST] + [(8, k) for k in range(KD)]
ADA_CD = {CD0 + 3: 2, CD0 + 4: 2, CD0 + 5: 2, CD0 + 6: 2, CD0 + 7: 2, CD0 + 8: 2, CD0 + 9: 2}
ADA_TILES += [(11, k) for k in REST]
LATE1 = len(REST)
ADA_FF1 = len(ADA_TILES)
Y_PAIRS = ((8, 9), (10, 11), (0, 1), (2, 3), (4, 5), (6, 7))


def val(const, i=None, per=0):
    return const if i is None else i * per + const


class Steps:

    def __init__(self, eng, sem):
        self.eng, self.sem, self.n, self.i, self.per = eng, sem, 0, None, 0

    def done(self, ins):
        ins.then_inc(self.sem, 1)
        self.n += 1
        return val(self.n, self.i, self.per)

    def wait(self, value):
        self.eng.wait_ge(self.sem, value)

    def link(self, ins):
        self.wait(self.done(ins))

    def enter(self, i, per):
        self.first, self.i, self.per = self.n, i, per

    def leave(self, turns):
        assert self.n - self.first == self.per, (self.n - self.first, self.per)
        self.n, self.i = self.first + turns * self.per, None


def trunk(nc, x, c, positions, ab_w_in, ab_vnorm_g, ab_vnorm_b, ab_spatial_w, ab_spatial_b,
          ab_pool_w, ab_pool_scale, ab_w_out, cd_w_in, cd_conv_w, cd_w_out, ffn_w_up, ffn_conv_w,
          ffn_w_down, ada_w, ada_b, norm_g, out):
    with ExitStack() as ctx:
        def sb(name, shape, dt=F32):
            return ctx.enter_context(nc.sbuf_tensor(name, shape, dt))

        def sem(name):
            return ctx.enter_context(nc.semaphore(name))

        def overlay(name, size, *groups):
            made = []
            for group in groups:
                with ExitStack() as inner:
                    made += [inner.enter_context(nc.sbuf_tensor(*t)) for t in group]
            sb(name, [P, size])
            return made

        raw = sb("raw", [P, RAW, TILE])
        w_hi = sb("w_hi", [P, RING, TILE], F32R)
        w_lo = sb("w_lo", [P, RING, TILE], F32R)
        ada = sb("ada", [P, 2, D])
        xs = sb("xs", [P, NT, D])
        hT_hi = sb("hT_hi", [P, KD, TOK], F32R)
        hT_lo = sb("hT_lo", [P, KD, TOK], F32R)
        gate = sb("gate", [P, D])
        acc = sb("acc", [P, 3, D])
        tmp = sb("tmp", [P, 4, TOK])
        ident = sb("ident", [P, P])
        ones = sb("ones", [P, 1])
        cols = sb("cols", [P, R_ALL])
        ffn_cols = sb("ffn_cols", [P, 3, 2 * 2 * FCH])
        mod = sb("mod", [P, 4, 2, KD])
        cact = sb("cact", [P, KD])
        zero = sb("zero", [1, P], BF16)
        sums = sb("sums", [P, 16])
        rstd = sb("rstd", [P, 18])
        nhalf = sb("nhalf", [P, 2])
        cnt_i = sb("cnt_i", [P, PAD], I32)
        cnt_f = sb("cnt_f", [P, PAD])
        inv_cnt = sb("inv_cnt", [P, NB, PAD])
        pos_i = sb("pos_i", [P, NT], I32)
        pos_f = sb("pos_f", [P, NT])
        inv_freq = sb("inv_freq", [P, HALF])
        angle = sb("angle", [P, NT * HALF])
        turns_i = sb("turns_i", [P, 2, NT * HALF], I32)
        turns_f = sb("turns_f", [P, 2, NT * HALF])
        trig = sb("trig", [P, 2, NT, HALF])
        v_stat = sb("v_stat", [P, NT, 2, 6])
        v_mv = sb("v_mv", [P, NT, 2])
        s_min = sb("s_min", [P, 2, 2])
        s_sum = sb("s_sum", [P, 2, 2])
        ws_raw, small_rows, conv_rows, c_rows, pool_x, pool_a, pool_b, yTa_hi, yTa_lo = overlay(
            "place_y", 16 * TOK,
            [("ws_raw", [P, A_GROUPS, P], F32), ("small_rows", [R_ALL, P], F32), ("conv_rows", [4 * FCH, 3, P], F32),
             ("c_rows", [KD, P], F32)],
            [("pool_x", [P, NB, PAD + TOK], F32), ("pool_a", [P, NB, PAD + TOK], F32), ("pool_b", [P, NB - 1, PAD + TOK], F32)],
            [("yTa_hi", [P, KD, TOK], F32R), ("yTa_lo", [P, KD, TOK], F32R)])
        yTb_hi, yTb_lo, ccs, cm, cy = overlay(
            "place_b", 8 * TOK,
            [("yTb_hi", [P, NB, TOK], F32R), ("yTb_lo", [P, NB, TOK], F32R)],
            [("ccs", [P, 2, TOK], F32), ("cm", [P, 2, TOK], F32), ("cy", [P, 2, TOK], F32)])
        xh, vn, cbuf, qk = overlay(
            "place_x", NT * D,
            [("xh", [P, NT, D], F32)], [("vn", [P, NT, A_WIDTH], F32)],
            [("cbuf", [P, 2, 2, 2 * TOK], F32)], [("qk", [P, 2, NT, HEADS * HD], F32)])
        vg, vb, bs, wsT, pool_w, gu, mx, accs, vs, qT, kT, prob, probT, mask = overlay(
            "place_m", 24 * TOK,
            [("vg", [P, D], F32), ("vb", [P, D], F32), ("bs", [P, A_GROUPS, P], F32),
             ("wsT", [P, A_GROUPS, P], F32), ("pool_w", [P, NB, P], F32),
             ("gu", [P, 2, 2 * TOK], F32), ("mx", [P, 2 * TOK], F32)],
            [("accs", [P, 2, D], F32)],
            [("vs", [P, NT, HEADS * HD], F32), ("qT", [P, 4, TOK], F32), ("kT", [P, 4, TOK], F32),
             ("prob", [P, 2, 3 * P], F32), ("probT", [P, 2, 3 * P], F32), ("mask", [P, 3 * P], F32)])
        ps = ctx.enter_context(nc.psum_tensor("ps", [P, 8, 512], F32))

        raw_in = [sem(f"raw_in{i}") for i in range(RAW)]
        ada_in = [sem(f"ada_in{i}") for i in range(2)]
        x_in = sem("x_in")
        c_in = sem("c_in")
        pos_in = sem("pos_in")
        rows_in = sem("rows_in")
        bias_in = [sem(f"bias_in{v}") for v in range(12)]
        ws_in = sem("ws_in")
        ab_in = sem("ab_in")
        grow_in = sem("grow_in")
        out_done = sem("out_done")
        hi_done = sem("hi_done")
        lo_dve = sem("lo_dve")
        lo_pool = sem("lo_pool")
        tile_used = sem("tile_used")
        ada_step = sem("ada_step")
        act_step = sem("act_step")
        dve_step = sem("dve_step")
        pool_step = sem("pool_step")
        consts_ready = sem("consts_ready")
        cT_ps = sem("cT_ps")
        rowsT_ps = sem("rowsT_ps")
        wsT_ps = sem("wsT_ps")
        ws_masked = sem("ws_masked")
        small_ready = sem("small_ready")
        wsT_ready = sem("wsT_ready")
        cact_ready = sem("cact_ready")
        angles_ready = sem("angles_ready")
        trig_ready = sem("trig_ready")
        col_ps = sem("col_ps")
        mod_ready = sem("mod_ready")
        gate_ps = sem("gate_ps")
        gate_ready = sem("gate_ready")
        sq_done = sem("sq_done")
        rs_done = sem("rs_done")
        xh_done = sem("xh_done")
        xT_ps = sem("xT_ps")
        hf_done = sem("hf_done")
        h_done = sem("h_done")
        x_ready = sem("x_ready")
        y_ps = sem("y_ps")
        v_ready = sem("v_ready")
        v_var = sem("v_var")
        v_rstd = sem("v_rstd")
        vn_ready = sem("vn_ready")
        cnt_ready = sem("cnt_ready")
        px_ready = sem("px_ready")
        pooled = sem("pooled")
        poolmix_ps = sem("poolmix_ps")
        yb_f = sem("yb_f")
        gu_ready = sem("gu_ready")
        mix_ps = sem("mix_ps")
        y_ready = sem("y_ready")
        yb_ready = sem("yb_ready")
        up_free = sem("up_free")
        tap_done = sem("tap_done")
        silu_done = sem("silu_done")
        aT_ready = sem("aT_ready")
        qkv_s = sem("qkv_s")
        rot_done = sem("rot_done")
        qkT_ps = sem("qkT_ps")
        qkT_ready = sem("qkT_ready")
        ccs_ready = sem("ccs_ready")
        cm_ready = sem("cm_ready")
        ctap_done = sem("ctap_done")
        yc_ready = sem("yc_ready")
        mask_ready = sem("mask_ready")
        score_ps = sem("score_ps")
        min_ready = sem("min_ready")
        exp_done = sem("exp_done")
        prob_ready = sem("prob_ready")
        probT_ps = sem("probT_ps")
        probT_ready = sem("probT_ready")
        pv_ps = sem("pv_ps")
        yd_ready = sem("yd_ready")

        ab_in_w = ab_w_in[0].rearrange("(k p) n -> p k n", p=P)
        ab_out_w = ab_w_out[0].rearrange("(k p) n -> p k n", p=P)
        cd_in_w = cd_w_in[0].rearrange("(k p) n -> p k n", p=P)
        cd_out_w = cd_w_out[0].rearrange("(k p) n -> p k n", p=P)
        up_w = [ffn_w_up[l].rearrange("(k p) n -> p k n", p=P) for l in range(2)]
        down_w = [ffn_w_down[l].rearrange("(k p) n -> p k n", p=P) for l in range(2)]
        ada_v = [ada_w[l].rearrange("(k p) n -> p k n", p=P) for l in range(2)]
        x_v = x[0].rearrange("(t p) d -> p t d", p=P)
        out_v = out[0].rearrange("(t p) d -> p t d", p=P)

        def mixer_tile(n):
            if n < FF0:
                if n < 4:
                    return ab_in_w[:, 4 * (n % 2):4 * (n % 2) + 4, A_WIDTH + 512 * (n // 2):A_WIDTH + 512 * (n // 2) + 512]
                if n < 6:
                    return ab_in_w[:, :, 2 * A_WIDTH + 256 * (n - 4):2 * A_WIDTH + 256 * (n - 3)]
                if n < 10:
                    return ab_in_w[:, :, 256 * (n - 6):256 * (n - 5)]
                k = Y_PAIRS[n - 10][0]
                return ab_out_w[:, k:k + 2, :]
            n -= CD0
            if n < 6:
                c0 = 3 * C_WIDTH + 512 * (n // 2)
                return cd_in_w[:, 4 * (n % 2):4 * (n % 2) + 4, c0:c0 + 512]
            if n < 12:
                c0 = (C_WIDTH, 2 * C_WIDTH, 0)[n % 3] + 256 * ((n - 6) // 3)
                return cd_in_w[:, :, c0:c0 + 256]
            return cd_out_w[:, 2 * (n - 12):2 * (n - 12) + 2, :]

        def as_k4(w, slot):
            return w[:, slot, :].rearrange("p (k n) -> p k n", k=4)

        def as_k8(w, slot):
            return w[:, slot, :].rearrange("p (k n) -> p k n", k=8)

        def as_k2(w, slot):
            return w[:, slot, :].rearrange("p (k n) -> p k n", k=2)

        def y_of(t):
            return ps[:, 4 + 2 * t:6 + 2 * t, :].rearrange("p b n -> p (b n)")

        acc_of = {v: acc[:, slot, :] for v, slot in
                  {0: 0, 1: 1, 2: 2, 3: 0, 4: 1, 5: 2, 9: 0, 10: 1, 8: 2, 11: 2}.items()}
        acc_of.update({6: accs[:, 0, :], 7: accs[:, 1, :]})

        block = ctx.enter_context(nc.Block())

        @block.sync
        def _(sp):
            def weights(n, i, src, k):
                m = n + PRO
                if n >= RAW:
                    sp.wait_ge(lo_dve, val(n - RAW + 1, i, 6))
                    sp.wait_ge(lo_pool, val(n - RAW + 1, i, 6))
                elif m >= RAW:
                    sp.wait_ge(ada_step, 2 * (m - RAW) + 2)
                dst = raw[:, m % RAW, :].rearrange("p (k n) -> p k n", k=k)
                sp.dma_start(dst, src).then_inc(raw_in[m % RAW], 16)

            def ada_src(v, k):
                return ada_v[v // 6][:, k, (v % 6) * D:(v % 6 + 1) * D]

            def ada_tile(a, i, src):
                if a >= 2:
                    sp.wait_ge(ada_step, val(2 * PRO + a - 1, i, 4))
                sp.dma_start(ada[:, a % 2, :], src).then_inc(ada_in[a % 2], 16)

            a_next = [0]

            def ada_tiles(count):
                for _ in range(count):
                    ada_tile(a_next[0], None, ada_src(*ADA_TILES[a_next[0]]))
                    a_next[0] += 1

            def straight(first, last, table):
                for n in range(first, last):
                    src = mixer_tile(n)
                    weights(n, None, src, src.shape[1])
                    ada_tiles(table.get(n - 3, 0))

            for m in range(PRO):
                if m >= RAW:
                    sp.wait_ge(ada_step, 2 * (m - RAW) + 2)
                v, k = m // 4, 2 * (m % 4)
                sp.dma_start(raw[:, m % RAW, :].rearrange("p (k n) -> p k n", k=2),
                             ada_v[0][:, k:k + 2, v * D:(v + 1) * D]).then_inc(raw_in[m % RAW], 16)
                if m == 3:
                    sp.dma_start(xs[:, :, :], x_v).then_inc(x_in, 16)
            sp.dma_start(ws_raw[:, :, :], ab_spatial_w[0].rearrange("g i j -> i g j")).then_inc(ws_in, 16)
            straight(AB0, 4, ADA_AB)
            for t, src in ((vg, ab_vnorm_g[0]), (vb, ab_vnorm_b[0])):
                sp.dma_start(t[:, :], src.partition_broadcast(P)).then_inc(ab_in, 16)
            sp.dma_start(bs[:, :, :].rearrange("p g i -> p (g i)"),
                         ab_spatial_b[0].rearrange("g i -> (g i)").partition_broadcast(P)).then_inc(ab_in, 16)
            sp.dma_start(pool_w[:, :, :], ab_pool_w[0].rearrange("g d e -> d g e")).then_inc(ab_in, 16)
            straight(4, 10, ADA_AB)
            sp.dma_start(gate[:, :], norm_g[0, 1].partition_broadcast(P)).then_inc(grow_in, 16)
            straight(10, FF0, ADA_AB)

            def ffn(l, base):
                table = (ADA_AB, {})[l]

                def up(s_col, n, i):
                    weights(n, i, up_w[l][:, :, s_col], KD)

                def step_weights(c, i, first):
                    up(bass.ds(val(256 * first, i, 512), 256), c, i)
                    up(bass.ds(val(FF + 256 * first, i, 512), 256), c + 1, i)
                    weights(c + 2, i, down_w[l][:, bass.ds(val(2 * first - 2, i, 4), 2), :], 2)

                def loop_ada(i, r):
                    if l == 0:
                        for j in range(2):
                            v = LOOP_V[2 * r + j] - 6
                            src = ada_v[1][:, bass.ds(i, 1), v * D:(v + 1) * D].rearrange("p o n -> p (o n)")
                            ada_tile(ADA_FF + 2 * r + j, i, src)
                    elif r == 0:
                        sp.wait_ge(ada_step, val(2 * PRO + ADA_FF1, i, 1))
                        sp.dma_start(ada[:, 1, :], ada_v[1][:, bass.ds(i, 1), 5 * D:6 * D].rearrange("p o n -> p (o n)")).then_inc(ada_in[1], 16)

                up(slice(0, 256), base, None)
                ada_tiles(table.get(base - 3, 0))
                up(slice(FF, FF + 256), base + 1, None)
                ada_tiles(table.get(base - 2, 0))
                step_weights(base + 2, None, 1)
                ada_tiles(table.get(base - 1, 0) + table.get(base, 0) + table.get(base + 1, 0) + (LATE0, LATE1)[l])
                with sp.Fori(0, 4) as i:
                    for r in range(2):
                        step_weights(base + 5 + 3 * r, i, 2 + r)
                        loop_ada(i, r)
                step_weights(base + 29, None, STEPS - 1)
                last_ada(l, 0)
                weights(base + 32, None, down_w[l][:, 2 * STEPS - 2:2 * STEPS, :], 2)
                if l == 0:
                    weights(CD0, None, mixer_tile(CD0), 4)
                    last_ada(l, 1)
                    weights(CD0 + 1, None, mixer_tile(CD0 + 1), 4)

            def last_ada(l, r):
                k = LOOP_K - 1
                if l == 0:
                    for j in range(2):
                        ada_tile(ADA_FF + 4 * k + 2 * r + j, None, ada_src(LOOP_V[2 * r + j], k))
                else:
                    sp.wait_ge(ada_step, 2 * PRO + ADA_FF1 + k)
                    sp.dma_start(ada[:, 1, :], ada_src(11, k)).then_inc(ada_in[1], 16)

            ffn(0, FF0)
            a_next[0] = ADA_MID
            straight(CD0 + 2, FF1, ADA_CD)
            ffn(1, FF1)
            for t in range(NT):
                sp.wait_ge(x_ready, 2 * 3 + t + 1)
                sp.dma_start(out_v[:, t, :], xs[:, t, :]).then_inc(out_done, 16)
            sp.wait_ge(out_done, 16 * NT)

        @block.gpsimd
        def _(pool):
            st = Steps(pool, pool_step)

            def split_lo(n, i=None):
                pool.wait_ge(hi_done, val(n + 1, i, 6))
                pool.tensor_tensor(w_lo[:, n % RING, LO_DVE:TILE], raw[:, (n + PRO) % RAW, LO_DVE:TILE],
                                   w_hi[:, n % RING, LO_DVE:TILE].bitcast(F32), ALU.subtract).then_inc(lo_pool, 1)

            def inv_rms(src, dst, scale):
                st.link(pool.tensor_scalar(dst, src, scale, EPS, ALU.mult, ALU.add))
                return pool.tensor_tensor(dst, dst, nhalf[:, 0:1], ALU.pow)

            def boundary(r):
                for t in range(NT):
                    pool.wait_ge(sq_done, 4 * r + t + 3)
                    j = 4 * r + t + 2
                    inv_rms(sums[:, j:j + 1], rstd[:, j:j + 1], 1.0 / D).then_inc(rs_done, 1)
                if r < 3:
                    norm(r + 1)

            def norm(m):
                for t in range(NT):
                    pool.wait_ge(sq_done, 4 * m + t + 1)
                    j = 4 * m + t
                    inv_rms(sums[:, j:j + 1], rstd[:, j:j + 1], 1.0 / D).then_inc(rs_done, 1)

            def start_acc(*vs):
                for v in vs:
                    last = st.done(pool.memset(acc_of[v], 0.0))
                for v in vs:
                    st.wait(last)
                    pool.dma_start(acc_of[v][0:1, :], ada_b[v // 6:v // 6 + 1, (v % 6) * D:(v % 6 + 1) * D]).then_inc(bias_in[v], 16)

            st.link(pool.memset(ident[:, :], 0.0))
            pool.affine_select(out=ident[:, :], in_=ident[:, :], compare_op=ALU.not_equal, fill=1.0, base=0,
                               pattern=[[-1, P]], channel_multiplier=1).then_inc(consts_ready, 1)
            start_acc(0)
            start_acc(1, 2)
            pool.memset(ones[:, :], 1.0).then_inc(consts_ready, 1)
            pool.memset(zero[:, :], 0.0).then_inc(consts_ready, 1)
            st.link(pool.memset(nhalf[:, :], -0.5))
            freq = np.float32(500000.0) ** (-np.arange(0, ROT, 2, dtype=np.float32) / np.float32(ROT))
            for j in range(HALF):
                pool.memset(inv_freq[:, j:j + 1], float(freq[j])).then_inc(consts_ready, 1)
            pool.iota(cnt_i[:, :], pattern=[[1, PAD]], base=1, channel_multiplier=0).then_inc(consts_ready, 1)
            norm(0)
            pool.wait_ge(ws_in, 16)
            pool.affine_select(out=ws_raw[:, :, :], in_=ws_raw[:, :, :], compare_op=ALU.is_ge, fill=0.0, base=0,
                               pattern=[[0, A_GROUPS], [-1, P]], channel_multiplier=1).then_inc(ws_masked, 1)
            for n in range(3):
                split_lo(n)
            pool.wait_ge(col_ps, 2)
            start_acc(3, 4)
            for n in range(3, 7):
                split_lo(n)
            pool.wait_ge(v_var, 1)
            for t in range(NT):
                inv_rms(v_mv[:, t, 1:2], rstd[:, 16 + t:17 + t], 1.0).then_inc(v_rstd, 1)
            split_lo(7)
            split_lo(8)
            pool.wait_ge(px_ready, 3)
            W = PAD + TOK
            st.link(pool.tensor_tensor(pool_a[:, :, 1:W], pool_x[:, :, 1:W], pool_x[:, :, 0:W - 1], ALU.add))
            st.link(pool.tensor_tensor(pool_b[:, :, 3:W], pool_a[:, 1:4, 3:W], pool_a[:, 1:4, 1:W - 2], ALU.add))
            st.link(pool.tensor_tensor(pool_a[:, 2:4, 7:W], pool_b[:, 1:3, 7:W], pool_b[:, 1:3, 3:W - 4], ALU.add))
            st.link(pool.tensor_tensor(pool_b[:, 2:3, 15:W], pool_a[:, 3:4, 15:W], pool_a[:, 3:4, 7:W - 8], ALU.add))
            split_lo(9)
            pool.wait_ge(cnt_ready, NB)
            for g, w in enumerate(WINDOWS):
                s = (pool_a[:, 0, :], pool_b[:, 0, :], pool_a[:, 2, :], pool_b[:, 2, :])[g]
                st.done(pool.tensor_tensor(s[:, PAD:2 * PAD], s[:, PAD:2 * PAD], inv_cnt[:, g, :], ALU.mult))
                st.link(pool.tensor_scalar(s[:, 2 * PAD:W], s[:, 2 * PAD:W], 1.0 / w, None, ALU.mult))
                pool.tensor_tensor(s[:, PAD:W], s[:, PAD:W], pool_x[:, g, PAD:W], ALU.subtract).then_inc(pooled, 1)
            for n in range(10, FF0 + 2):
                split_lo(n)
                if n == 14:
                    pool.wait_ge(gate_ps, 1)
                    start_acc(5)
                    pool.wait_ge(y_ready, 4)
                    start_acc(6, 7)
            pool.wait_ge(col_ps, 4)
            start_acc(9, 10)
            boundary(0)

            def ffn(l, base):
                with pool.Fori(0, 5) as i:
                    for c in range(6):
                        split_lo(base + 2 + c, i)
                split_lo(base + 32)
                if l == 0:
                    split_lo(base + 33)
                    split_lo(base + 34)

            ffn(0, FF0)
            boundary(1)
            pool.wait_ge(gate_ps, 2)
            start_acc(8)
            pool.wait_ge(col_ps, 6)
            st.link(pool.memset(mask[:, :], 0.0))
            for b in (0, 2):
                m = mask[:, b * P:(b + 1) * P]
                pool.affine_select(out=m, in_=m, compare_op=ALU.is_ge, fill=BIG, base=0, pattern=[[-1, P]],
                                   channel_multiplier=1).then_inc(mask_ready, 1)
            for n in range(CD0 + 2, FF1 + 2):
                split_lo(n)
            pool.wait_ge(gate_ps, 3)
            start_acc(11)
            boundary(2)
            ffn(1, FF1)
            boundary(3)

        @block.scalar
        def _(act):
            st = Steps(act, act_step)

            def split_hi(n, i=None):
                m = n + PRO
                act.wait_ge(raw_in[m % RAW], val(16 * (m // RAW + 1), i, 16))
                if n >= RING:
                    act.wait_ge(tile_used, val(n - RING + 1, i, 6))
                act.activation(w_hi[:, n % RING, :], raw[:, m % RAW, :], ACT.Copy).then_inc(hi_done, 1)

            def squares_of_x(m):
                for t in range(NT):
                    if m == 0:
                        act.wait_ge(x_in, 16)
                    else:
                        act.wait_ge(x_ready, 2 * (m - 1) + t + 1)
                    j = 4 * m + t
                    act.activation(xh[:, t, :], xs[:, t, :], ACT.Square,
                                   accum_out=sums[:, j:j + 1]).then_inc(sq_done, 1)

            def shift_scale(m):
                act.wait_ge(mod_ready, m + 1)
                for b in range(4):
                    act.wait_ge(xT_ps, 4 * m + b + 1)
                    if b >= 2:
                        act.wait_ge(h_done, 4 * m + b - 1)
                    for a in range(2):
                        k = 2 * b + a
                        ins = act.activation(tmp[:, 2 * (b % 2) + a, :], ps[:, b, a * TOK:(a + 1) * TOK], ACT.Identity,
                                             scale=mod[:, m, 1, k:k + 1], bias=mod[:, m, 0, k:k + 1])
                    ins.then_inc(hf_done, 1)

            def squares_of_y(r):
                for t in range(NT):
                    if t == 0:
                        act.wait_ge(y_ps, r + 1)
                    else:
                        act.wait_ge(tile_used, (FF0, CD0, FF1, END)[r])
                    j = 4 * r + t + 2
                    junk = hT_lo[:, 4 * t:4 * t + 4, :].rearrange("p k t -> p (k t)")
                    act.activation(junk, y_of(t), ACT.Square, accum_out=sums[:, j:j + 1]).then_inc(sq_done, 1)

            def gain_row(r):
                act.wait_ge(x_ready, 2 * r)
                act.dma_start(gate[:, :], norm_g[r // 2, 1 + 2 * (r % 2)].partition_broadcast(P)).then_inc(grow_in, 16)

            act.dma_start(c_rows[:, :], c.rearrange("o (k p) -> (o k) p", p=P)).then_inc(c_in, 16)
            act.dma_start(small_rows[R_NORM:R_POOL, :], norm_g.rearrange("l n (k p) -> (l n k) p", p=P)).then_inc(rows_in, 16)
            act.dma_start(small_rows[R_POOL:R_CONV, :], ab_pool_scale.rearrange("o (k p) -> (o k) p", p=P)).then_inc(rows_in, 16)
            act.dma_start(small_rows[R_CONV:R_ALL, :], cd_conv_w.rearrange("o t (k p) -> (o t k) p", p=P)).then_inc(rows_in, 16)
            act.wait_ge(cT_ps, 1)
            act.activation(cact[:, :], ps[:, 4, 0:KD], ACT.Silu).then_inc(cact_ready, 1)
            for l in range(2):
                act.dma_start(conv_rows[2 * FCH * l:2 * FCH * (l + 1), :, :],
                              ffn_conv_w[l].rearrange("t (k p) -> k t p", p=P)).then_inc(rows_in, 16)
            act.dma_start(pos_i[:, :], positions.rearrange("o (t p) -> p (o t)", p=P),
                          allow_slow_non_contiguous=True).then_inc(pos_in, 16)
            act.wait_ge(rowsT_ps, 1)
            act.activation(cols[:, :], ps[:, 0, 0:R_ALL], ACT.Copy).then_inc(small_ready, 1)
            act.activation(ffn_cols[:, :, :].rearrange("p t k -> p (t k)"), ps[:, 1, 0:12 * FCH], ACT.Copy).then_inc(small_ready, 1)
            squares_of_x(0)
            split_hi(0)
            shift_scale(0)
            split_hi(1)
            act.wait_ge(wsT_ps, 1)
            act.activation(wsT[:, :, :].rearrange("p (b g) i -> p b (g i)", b=2), ps[:, 6:8, :], ACT.Copy).then_inc(wsT_ready, 1)
            split_hi(2)

            for n in range(AB0, FF0):
                if n < FF0 - 1:
                    split_hi(n + RING)
                if n == 2:
                    act.wait_ge(angles_ready, 1)
                    act.activation(trig[:, :, :, :].rearrange("p s t j -> p (s t j)"),
                                   turns_f[:, :, :].rearrange("p s j -> p (s j)"), ACT.Sin).then_inc(trig_ready, 1)
                if n == 1 or n == 3:
                    b = 4 + (n // 2) * 2
                    h = n // 2
                    act.wait_ge(tile_used, n + 1)
                    act.activation(vn[:, :, 512 * h:512 * h + 512], ps[:, b:b + 2, :], ACT.Gelu_apprx_tanh).then_inc(v_ready, 1)
                if n in (4, 5):
                    act.wait_ge(tile_used, n + 1)
                    act.activation(pool_x[:, 2 * (n - 4):2 * (n - 4) + 2, PAD:PAD + TOK],
                                   ps[:, n - 4, :].rearrange("p (a t) -> p a t", a=2), ACT.Copy).then_inc(px_ready, 1)
                if 6 <= n < 10:
                    j = n - 6
                    act.wait_ge(tile_used, n + 1)
                    if j >= 2:
                        act.wait_ge(y_ready, j - 1)
                    act.activation(gu[:, j % 2, :], ps[:, (2, 0)[j % 2], :], ACT.Gelu_apprx_tanh).then_inc(gu_ready, 1)
                if n == 8:
                    act.wait_ge(poolmix_ps, 1)
                    for g in range(NB):
                        ins = act.activation(tmp[:, g, :], ps[:, 6 + g // 2, (g % 2) * TOK:(g % 2 + 1) * TOK], ACT.Copy,
                                             scale=cols[:, R_POOL + g:R_POOL + g + 1])
                    ins.then_inc(yb_f, 1)

            def ffn(l, base):
                W2 = 2

                def taps(k, i, par):
                    act.wait_ge(aT_ready, val(13 * l + k + 1, i, 2))
                    for h in range(2):
                        act.wait_ge(tile_used, base + 3 * k + h if i is None else val(base + 3 * k + h + 1, i, 6))
                        for a in range(2):
                            col = 2 * FCH * l + FCH * h + 2 * k + a
                            ins = act.activation(cbuf[:, par, h, a * TOK:(a + 1) * TOK],
                                                 ps[:, 2 * par + h, a * TOK:(a + 1) * TOK], ACT.Copy,
                                                 scale=ffn_cols[:, W2, bass.ds(val(col, i, 4), 1)])
                        ins.then_inc(tap_done, 1)

                def silu(k, i, par):
                    act.wait_ge(up_free, val(26 * l + 4 + 2 * k + 1, i, 4))
                    act.activation(cbuf[:, par, 0, :], cbuf[:, par, 0, :], ACT.Silu).then_inc(silu_done, 1)

                with act.Fori(0, 5) as i:
                    for r in range(2):
                        split_hi(base + 2 + 3 * r, i)
                        taps(r, i, r)
                        split_hi(base + 3 + 3 * r, i)
                        silu(r, i, r)
                        split_hi(base + 4 + 3 * r, i)
                split_hi(base + 32)
                taps(10, None, 0)
                silu(10, None, 0)
                if l == 0:
                    split_hi(base + 33)
                    split_hi(base + 34)

            squares_of_y(0)
            squares_of_x(1)
            shift_scale(1)
            gain_row(1)
            ffn(0, FF0)
            squares_of_y(1)
            squares_of_x(2)
            shift_scale(2)
            gain_row(2)
            split_hi(CD0 + 2)

            def exps(h):
                act.wait_ge(min_ready, h + 1)
                for q in range(NT):
                    s = prob[:, h % 2, (0, P)[q]:(P, 3 * P)[q]]
                    ins = act.activation(s, s, ACT.Exp, scale=-1.0, bias=s_min[:, h % 2, q:q + 1],
                                         accum_out=s_sum[:, h % 2, q:q + 1])
                ins.then_inc(exp_done, 1)

            def move_probT(h):
                act.wait_ge(probT_ps, h + 1)
                if h >= 2:
                    act.wait_ge(pv_ps, h - 1)
                act.activation(probT[:, h % 2, :], ps[:, 6 + h % 2, 0:3 * P], ACT.Copy).then_inc(probT_ready, 1)

            def ctaps(j):
                act.wait_ge(cm_ready, j + 1)
                if j:
                    act.wait_ge(yc_ready, j)
                for a in range(2):
                    col = R_CONV + 4 * 2 + 2 * j + a
                    ins = act.activation(cy[:, a, :], cm[:, a, :], ACT.Copy, scale=cols[:, col:col + 1])
                ins.then_inc(ctap_done, 1)

            for n in range(16):
                if n < 15:
                    split_hi(CD0 + n + RING)
                used = CD0 + n + 1
                if n in (1, 3, 5):
                    act.wait_ge(tile_used, used)
                    b = (4, 6, 0)[n // 2]
                    dst = vs[:, :, :] if n == 5 else qk[:, n // 2, :, :]
                    act.activation(dst, ps[:, b:b + 2, :], ACT.Copy).then_inc(qkv_s, 1)
                if n == 6:
                    act.wait_ge(tile_used, used)
                    act.activation(ccs[:, :, :].rearrange("p a t -> p (a t)"), ps[:, 2, :], ACT.Copy).then_inc(ccs_ready, 1)
                    for z, dst in enumerate((qT, kT)):
                        act.wait_ge(qkT_ps, z + 1)
                        act.activation(dst[:, :, :].rearrange("p (b a) t -> p b (a t)", b=2), ps[:, 4 + 2 * z:6 + 2 * z, :],
                                       ACT.Copy).then_inc(qkT_ready, 1)
                if n == 7:
                    ctaps(0)
                    exps(0)
                    exps(1)
                if n == 8:
                    move_probT(0)
                    move_probT(1)
                    exps(2)
                    exps(3)
                if n == 9:
                    act.wait_ge(tile_used, used)
                    act.wait_ge(cm_ready, 1)
                    act.activation(ccs[:, :, :].rearrange("p a t -> p (a t)"), ps[:, 2, :], ACT.Copy).then_inc(ccs_ready, 1)
                    move_probT(2)
                    move_probT(3)
                    exps(4)
                    exps(5)
                if n == 10:
                    ctaps(1)
                    move_probT(4)
                    move_probT(5)
                    exps(6)
                    exps(7)
                if n == 11:
                    move_probT(6)
                    move_probT(7)
            squares_of_y(2)
            squares_of_x(3)
            shift_scale(3)
            gain_row(3)
            ffn(1, FF1)
            squares_of_y(3)

        @block.tensor
        def _(pe):
            def need(n, i=None):
                pe.wait_ge(hi_done, val(n + 1, i, 6))
                pe.wait_ge(lo_dve, val(n + 1, i, 6))
                pe.wait_ge(lo_pool, val(n + 1, i, 6))

            def tile_T(n, bank, i=None):
                need(n, i)
                hi, lo = as_k8(w_hi, n % RING), as_k8(w_lo, n % RING)
                for a in range(2):
                    o = ps[:, bank, a * TOK:(a + 1) * TOK]
                    f = slice(a * P, (a + 1) * P)
                    for k in range(KD):
                        pe.matmul(o, hi[:, k, f], hT_hi[:, k, :], start=(k == 0), stop=False)
                        pe.matmul(o, hi[:, k, f], hT_lo[:, k, :], start=False, stop=False)
                        ins = pe.matmul(o, lo[:, k, f], hT_hi[:, k, :], start=False, stop=(k == KD - 1))
                ins.then_inc(tile_used, 1)

            def tile_M(n, bank):
                need(n)
                hi, lo = as_k4(w_hi, n % RING), as_k4(w_lo, n % RING)
                kh = (n - (CD0 if n >= CD0 else 0)) % 2
                for t in range(NT):
                    o = ps[:, bank + t, :]
                    f = slice(t * P, (t + 1) * P)
                    for k in range(4):
                        kk = 4 * kh + k
                        if n in (AB0, AB0 + 1, CD0, CD0 + 1) and t == 0 and k % 2 == 0:
                            pe.wait_ge(h_done, (0 if n < CD0 else 8) + kk // 2 + 1)
                        pe.matmul(o, hT_hi[:, kk, f], hi[:, k, :], start=(kk == 0), stop=False)
                        pe.matmul(o, hT_hi[:, kk, f], lo[:, k, :], start=False, stop=False)
                        ins = pe.matmul(o, hT_lo[:, kk, f], hi[:, k, :], start=False, stop=(kk == KD - 1))
                ins.then_inc(tile_used, 1)

            def tile_Y(n, y_hi, y_lo, first, last, i=None, done=None):
                need(n, i)
                hi, lo = as_k2(w_hi, n % RING), as_k2(w_lo, n % RING)
                for t in range(NT):
                    f = slice(t * P, (t + 1) * P)
                    for a in range(2):
                        for h in range(2):
                            o = ps[:, 4 + 2 * t + h, :]
                            cs = slice(512 * h, 512 * h + 512)
                            pe.matmul(o, y_hi[:, a, f], hi[:, a, cs], start=(first and a == 0), stop=False)
                            pe.matmul(o, y_hi[:, a, f], lo[:, a, cs], start=False, stop=False)
                            ins = pe.matmul(o, y_lo[:, a, f], hi[:, a, cs], start=False, stop=(last and a == 1))
                    if last and t == 0:
                        ins.then_inc(y_ps, 1)
                ins.then_inc(tile_used, 1)

            def column(v, col):
                for k in range(KD):
                    f = slice(k * P, (k + 1) * P)
                    ins = pe.matmul(ps[:, col[0], col[1] + k:col[1] + k + 1], acc_of[v][:, f], ones[:, 0:1], start=True, stop=True)
                ins.then_inc(col_ps, 1)

            def gate_rows(v):
                for h in range(2):
                    cs = slice(512 * h, 512 * h + 512)
                    ins = pe.matmul(ps[:, 2 + h, :], ones[:, 0:1].to_broadcast([P, P]), acc_of[v][:, cs], start=True, stop=True)
                ins.then_inc(gate_ps, 1)

            def transpose_x(m):
                pe.wait_ge(xh_done, 2 * m + 2)
                for b in range(4):
                    for a in range(2):
                        for t in range(NT):
                            f = slice((2 * b + a) * P, (2 * b + a + 1) * P)
                            ins = pe.transpose(ps[:, b, a * TOK + t * P:a * TOK + (t + 1) * P], xh[:, t, f], ident[:, :])
                    ins.then_inc(xT_ps, 1)

            pe.wait_ge(consts_ready, 1)
            pe.wait_ge(c_in, 16)
            pe.transpose(ps[:, 4, 0:KD], c_rows[:, :], ident[0:KD, 0:KD]).then_inc(cT_ps, 1)
            pe.wait_ge(rows_in, 16 * 5)
            pe.transpose(ps[:, 0, 0:R_ALL], small_rows[:, :], ident[0:R_ALL, 0:R_ALL])
            for t in range(3):
                ins = pe.transpose(ps[:, 1, 4 * FCH * t:4 * FCH * (t + 1)], conv_rows[:, t, :], ident[0:4 * FCH, 0:4 * FCH])
            ins.then_inc(rowsT_ps, 1)
            pe.wait_ge(small_ready, 2)
            transpose_x(0)
            pe.wait_ge(consts_ready, 3)
            for v in range(2):
                pe.wait_ge(ada_step, 8 * (v + 1))
                column(v, (5, KD * v))
            pe.wait_ge(ws_masked, 1)
            for g in range(A_GROUPS):
                ins = pe.transpose(ps[:, 6 + g // 4, (g % 4) * P:(g % 4 + 1) * P], ws_raw[:, g, :], ident[:, :])
            ins.then_inc(wsT_ps, 1)

            def mix(j, bank):
                if j == 0:
                    pe.wait_ge(vn_ready, 1)
                for a in range(2):
                    g = 2 * j + a
                    for t in range(NT):
                        ins = pe.matmul(ps[:, bank, a * TOK + t * P:a * TOK + (t + 1) * P],
                                        vn[:, t, g * P:(g + 1) * P], wsT[:, g, :], start=True, stop=True)
                ins.then_inc(mix_ps, 1)

            pe.wait_ge(mod_ready, 1)
            for n in range(4):
                if n == 2:
                    pe.wait_ge(wsT_ready, 1)
                tile_M(n, 4 + 2 * (n // 2))
            tile_T(4, 0)
            tile_T(5, 1)
            tile_T(6, 2)
            mix(0, 3)
            pe.wait_ge(px_ready, 3)
            tile_T(7, 0)
            mix(1, 1)
            pe.wait_ge(gu_ready, 1)
            tile_T(8, 2)
            pe.wait_ge(pooled, NB)
            pe.wait_ge(ab_in, 16 * 4)
            for g in range(NB):
                s = (pool_a[:, 0, :], pool_b[:, 0, :], pool_a[:, 2, :], pool_b[:, 2, :])[g]
                ins = pe.matmul(ps[:, 6 + g // 2, (g % 2) * TOK:(g % 2 + 1) * TOK], pool_w[:, g, :],
                                s[:, PAD:PAD + TOK], start=True, stop=True)
            ins.then_inc(poolmix_ps, 1)
            pe.wait_ge(y_ready, 1)
            mix(2, 3)
            pe.wait_ge(gu_ready, 2)
            tile_T(9, 0)
            pe.wait_ge(y_ready, 2)
            mix(3, 1)
            for n in range(10, FF0):
                pair = Y_PAIRS[n - 10]
                if pair[0] >= 8:
                    pe.wait_ge(yb_ready, 1)
                    y_hi, y_lo = yTb_hi[:, pair[0] - 8:pair[0] - 6, :], yTb_lo[:, pair[0] - 8:pair[0] - 6, :]
                else:
                    pe.wait_ge(y_ready, pair[0] // 2 + 1)
                    y_hi, y_lo = yTa_hi[:, pair[0]:pair[0] + 2, :], yTa_lo[:, pair[0]:pair[0] + 2, :]
                tile_Y(n, y_hi, y_lo, n == 10, n == FF0 - 1)
                if n == 11:
                    pe.wait_ge(ada_step, 2 * PRO + 8)
                    pe.wait_ge(y_ready, 3)
                    gate_rows(2)
                if n == 12:
                    pe.wait_ge(ada_step, 2 * PRO + 16)
                    pe.wait_ge(gu_ready, 4)
                    column(3, (0, 0))
                if n == 13:
                    pe.wait_ge(ada_step, 2 * PRO + 24)
                    column(4, (0, KD))

            def ffn(l, base):
                first = 26 * l
                pe.wait_ge(x_ready, 4 * l + 2)
                for b in range(4):
                    pe.matmul(ps[:, 4 + b, :], zero[:, :], zero[:, 0:1].to_broadcast([1, 512]), start=True, stop=False)
                pe.wait_ge(h_done, 8 * l + 8)
                for h in range(2):
                    pe.wait_ge(up_free, first + h + 1)
                    tile_T(base + h, h)
                with pe.Fori(0, 5) as i:
                    for r in range(2):
                        q = 1 - r
                        for h in range(2):
                            pe.wait_ge(up_free, val(first + 2 * (1 + r) + h + 1, i, 4))
                            tile_T(base + 2 + 3 * r + h, 2 * q + h, i)
                        pe.wait_ge(aT_ready, val(13 * l + 3 + r, i, 2))
                        tile_Y(base + 4 + 3 * r, yTa_hi[:, 2 * r:2 * r + 2, :], yTa_lo[:, 2 * r:2 * r + 2, :], False, False, i)
                pe.wait_ge(ada_step, 2 * PRO + (4 * KD if l == 0 else ADA_FF1 + LOOP_K))
                pe.wait_ge(up_free, first + 4 + 20)
                gate_rows(5 if l == 0 else 11)
                if l == 0:
                    pe.wait_ge(ada_step, 2 * PRO + ADA_MID - 2)
                    pe.wait_ge(up_free, first + 4 + 22)
                    for z, v in enumerate((6, 7)):
                        column(v, (0, KD * z))
                pe.wait_ge(aT_ready, 13 * l + 13)
                tile_Y(base + 32, yTa_hi[:, 0:2, :], yTa_lo[:, 0:2, :], False, True)

            transpose_x(1)
            ffn(0, FF0)
            pe.wait_ge(mod_ready, 3)
            pe.wait_ge(gate_ready, 2)
            transpose_x(2)

            def transpose_qk(z):
                pe.wait_ge(rot_done, z + 1)
                for k in range(4):
                    for t in range(NT):
                        o = ps[:, 4 + 2 * z + k // 2, (k % 2) * TOK + t * P:(k % 2) * TOK + (t + 1) * P]
                        ins = pe.transpose(o, qk[:, z, t, k * P:(k + 1) * P], ident[:, :])
                ins.then_inc(qkT_ps, 1)

            def scores(h):
                if h >= 2:
                    pe.wait_ge(min_ready, h - 1)
                r = slice(HD * (h % 2), HD * (h % 2) + HD)
                b = 4 + h % 2
                pe.matmul(ps[:, b, 0:P], qT[r, h // 2, 0:P], kT[r, h // 2, 0:P], start=True, stop=True)
                pe.matmul(ps[:, b, P:3 * P], qT[r, h // 2, P:TOK], kT[r, h // 2, :], start=True, stop=True).then_inc(score_ps, 1)

            def transpose_p(h):
                pe.wait_ge(prob_ready, h + 1)
                if h >= 2:
                    pe.wait_ge(probT_ready, h - 1)
                for b in range(3):
                    ins = pe.transpose(ps[:, 6 + h % 2, b * P:(b + 1) * P], prob[:, h % 2, b * P:(b + 1) * P], ident[:, :])
                ins.then_inc(probT_ps, 1)

            def values(h):
                pe.wait_ge(probT_ready, h + 1)
                if h >= 2:
                    pe.wait_ge(yd_ready, h // 2)
                r = slice(HD * (h % 2), HD * (h % 2) + HD)
                c0 = TOK * (h // 2 % 2)
                pe.matmul(ps[r, 1, c0:c0 + TOK], vs[:, 0, h * HD:(h + 1) * HD], probT[:, h % 2, 0:TOK], start=True, stop=False)
                pe.matmul(ps[r, 1, c0 + P:c0 + TOK], vs[:, 1, h * HD:(h + 1) * HD], probT[:, h % 2, TOK:3 * P],
                          start=False, stop=True).then_inc(pv_ps, 1)

            for n in range(2):
                tile_M(CD0 + n, 4)
            for n in range(2, 4):
                tile_M(CD0 + n, 6)
            pe.wait_ge(hf_done, 12)
            for n in range(4, 6):
                tile_M(CD0 + n, 0)
            tile_T(CD0 + 6, 2)
            transpose_qk(0)
            transpose_qk(1)
            tile_T(CD0 + 7, 3)
            pe.wait_ge(qkT_ready, 2)
            scores(0)
            scores(1)
            pe.wait_ge(qkv_s, 3)
            tile_T(CD0 + 8, 0)
            for h in (0, 1):
                transpose_p(h)
            for h in (2, 3):
                scores(h)
            pe.wait_ge(ccs_ready, 1)
            tile_T(CD0 + 9, 2)
            for h in range(2):
                values(h)
                transpose_p(h + 2)
                scores(h + 4)
            pe.wait_ge(cm_ready, 1)
            tile_T(CD0 + 10, 3)
            for h in range(2, 4):
                values(h)
                transpose_p(h + 2)
                scores(h + 4)
            pe.wait_ge(yc_ready, 1)
            tile_T(CD0 + 11, 0)
            for h in range(4, 6):
                values(h)
                transpose_p(h + 2)
            pe.wait_ge(probT_ready, 8)
            for n in range(12, 16):
                j = n - 12
                if j < 2:
                    pe.wait_ge(yc_ready, j + 1)
                else:
                    pe.wait_ge(yd_ready, 2 * (j - 1))
                tile_Y(CD0 + n, yTa_hi[:, 2 * j:2 * j + 2, :], yTa_lo[:, 2 * j:2 * j + 2, :], n == 12, n == 15)
                if n == 12:
                    values(6)
                    values(7)
                    pe.wait_ge(ada_step, 2 * PRO + ADA_FF1 - LATE1)
                    gate_rows(8)
                if n == 13:
                    for z, v in enumerate((9, 10)):
                        column(v, (0, KD * z))
            pe.wait_ge(mod_ready, 4)
            pe.wait_ge(gate_ready, 3)
            transpose_x(3)
            ffn(1, FF1)

        @block.vector
        def _(dve):
            st = Steps(dve, dve_step)
            a_next = [0]

            def split_lo(n, i=None):
                dve.wait_ge(hi_done, val(n + 1, i, 6))
                dve.tensor_tensor(w_lo[:, n % RING, 0:LO_DVE], raw[:, (n + PRO) % RAW, 0:LO_DVE],
                                  w_hi[:, n % RING, 0:LO_DVE].bitcast(F32), ALU.subtract).then_inc(lo_dve, 1)

            def ada_add(dst, src, k, before):
                if before is not None:
                    dve.wait_ge(ada_step, before)
                dve.scalar_tensor_tensor(dst, src, k, dst, ALU.mult, ALU.add).then_inc(ada_step, 1)

            def ada_tiles(count):
                for _ in range(count):
                    a = a_next[0]
                    v, k = ADA_TILES[a]
                    dve.wait_ge(ada_in[a % 2], 16 * (a // 2 + 1))
                    dve.wait_ge(bias_in[v], 16)
                    ada_add(acc_of[v], ada[:, a % 2, :], cact[:, k:k + 1], 2 * PRO + a)
                    a_next[0] += 1

            def split_both(src, hi, lo, signal):
                st.link(dve.tensor_copy(hi, src))
                dve.tensor_tensor(lo, src, hi.bitcast(F32), ALU.subtract).then_inc(signal, 1)

            def norm(m):
                for t in range(NT):
                    dve.wait_ge(rs_done, 4 * m + t + 1)
                    j = 4 * m + t
                    dve.tensor_scalar(xh[:, t, :], xs[:, t, :], rstd[:, j:j + 1], None, ALU.mult).then_inc(xh_done, 1)

            def split_h(m):
                for b in range(4):
                    dve.wait_ge(hf_done, 4 * m + b + 1)
                    split_both(tmp[:, 2 * (b % 2):2 * (b % 2) + 2, :], hT_hi[:, 2 * b:2 * b + 2, :],
                               hT_lo[:, 2 * b:2 * b + 2, :], h_done)

            def shift_and_scale(m, col):
                g0 = R_NORM + 32 * (m // 2) + 16 * (m % 2)
                sh = ps[:, col[0], col[1]:col[1] + KD]
                sc = ps[:, col[0], col[1] + KD:col[1] + 2 * KD]
                dve.tensor_copy(mod[:, m, 0, :], sh)
                return dve.scalar_tensor_tensor(mod[:, m, 1, :], sc, 1.0, cols[:, g0:g0 + KD], ALU.add, ALU.mult)

            def gate_mul(r):
                dve.wait_ge(gate_ps, r + 1)
                dve.wait_ge(grow_in, 16 * (r + 1))
                dve.tensor_tensor(gate[:, :], ps[:, 2:4, :].rearrange("p b n -> p (b n)"), gate[:, :],
                                  ALU.mult).then_inc(gate_ready, 1)

            def residual(r):
                dve.wait_ge(gate_ready, r + 1)
                for t in range(NT):
                    j = 4 * r + t + 2
                    yg = xh[:, t, :]
                    dve.wait_ge(sq_done, 4 * r + t + 3)
                    st.link(dve.tensor_tensor(yg, y_of(t), gate[:, :], ALU.mult))
                    dve.wait_ge(rs_done, 4 * r + t + 3)
                    dve.scalar_tensor_tensor(xs[:, t, :], yg, rstd[:, j:j + 1], xs[:, t, :], ALU.mult, ALU.add).then_inc(x_ready, 1)

            def constants():
                dve.wait_ge(consts_ready, 3 + HALF + 1)
                st.link(dve.tensor_copy(cnt_f[:, :], cnt_i[:, :]))
                for g, w in enumerate(WINDOWS):
                    last = st.done(dve.tensor_scalar_min(inv_cnt[:, g, :], cnt_f[:, :], float(w)))
                st.wait(last)
                for g in range(NB):
                    dve.reciprocal(inv_cnt[:, g, :], inv_cnt[:, g, :]).then_inc(cnt_ready, 1)
                dve.wait_ge(pos_in, 16)
                st.link(dve.tensor_copy(pos_f[:, :], pos_i[:, :]))
                for t in range(NT):
                    last = st.done(dve.tensor_scalar(angle[:, t * HALF:(t + 1) * HALF], inv_freq[:, :], pos_f[:, t:t + 1], None, ALU.mult))
                st.wait(last)
                two_pi = 2 * np.pi
                c1 = 6.28125
                c2 = float(np.float32(np.round((two_pi - c1) * 2 ** 21) / 2 ** 21))
                c3 = float(np.float32(two_pi - c1 - c2))
                for q in range(2):
                    last = st.done(dve.tensor_scalar(turns_i[:, q, :], angle[:, :], 1 / two_pi, 0.25 * q, ALU.mult, ALU.add))
                st.wait(last)
                kf = tmp[:, 0, 0:2 * NT * HALF].rearrange("p (q j) -> p q j", q=2)
                st.link(dve.tensor_copy(kf, turns_i[:, :, :]))
                for q in range(2):
                    last = st.done(dve.scalar_tensor_tensor(turns_f[:, q, :], kf[:, q, :], -c1, angle[:, :], ALU.mult, ALU.add))
                st.wait(last)
                for cc in (c2, c3):
                    st.link(dve.scalar_tensor_tensor(turns_f[:, :, :], kf, -cc, turns_f[:, :, :], ALU.mult, ALU.add))
                st.link(dve.tensor_scalar(turns_f[:, 1, :], turns_f[:, 1, :], float(np.pi / 2), None, ALU.add))
                pi_in = float(np.nextafter(np.float32(np.pi), np.float32(0)))
                dve.tensor_scalar(turns_f[:, :, :], turns_f[:, :, :], pi_in, -pi_in, ALU.min, ALU.max).then_inc(angles_ready, 1)

            dve.wait_ge(cact_ready, 1)
            for m in range(PRO):
                dve.wait_ge(raw_in[m % RAW], 16 * (m // RAW + 1))
                for j in range(2):
                    k = 2 * (m % 4) + j
                    if k == 0:
                        dve.wait_ge(bias_in[m // 4], 16)
                    ada_add(acc_of[m // 4], raw[:, m % RAW, j * D:(j + 1) * D], cact[:, k:k + 1], 2 * m + j or None)
                if m == 5:
                    norm(0)
            split_lo(0)
            dve.wait_ge(col_ps, 2)
            dve.wait_ge(small_ready, 1)
            shift_and_scale(0, (5, 0)).then_inc(mod_ready, 1)
            split_h(0)

            split_lo(1)
            dve.wait_ge(wsT_ps, 1)
            dve.memset(pool_x[:, :, 0:PAD], 0.0).then_inc(px_ready, 1)
            constants()
            split_lo(2)

            def mixed(j):
                bank = (3, 1)[j % 2]
                dve.wait_ge(mix_ps, j + 1)
                if j:
                    dve.wait_ge(y_ready, j)
                b = bs[:, 2 * j:2 * j + 2, None, :].to_broadcast([P, 2, NT, P])
                st.link(dve.tensor_tensor(mx[:, :].rearrange("p (g t i) -> p g t i", g=2, t=NT),
                                          ps[:, bank, :].rearrange("p (g t i) -> p g t i", g=2, t=NT), b, ALU.add))
                dve.wait_ge(gu_ready, j + 1)
                st.link(dve.tensor_tensor(mx[:, :], mx[:, :], gu[:, j % 2, :], ALU.mult))
                if j == 0:
                    dve.wait_ge(poolmix_ps, 1)
                m = mx[:, :].rearrange("p (a t) -> p a t", a=2)
                split_both(m, yTa_hi[:, 2 * j:2 * j + 2, :], yTa_lo[:, 2 * j:2 * j + 2, :], y_ready)

            for n in range(AB0, FF0):
                if n < FF0 - 1:
                    split_lo(n + RING)
                    ada_tiles(ADA_AB.get(n + RING, 0))
                if n in (1, 3):
                    h = n // 2
                    dve.wait_ge(v_ready, h + 1)
                    for t in range(NT):
                        last = st.done(dve.bn_stats(v_stat[:, t, h, :], vn[:, t, 512 * h:512 * h + 512]))
                if n == 3:
                    st.wait(last)
                    st.done(dve.bn_aggr(v_mv[:, 0, :], v_stat[:, 0, :, :]))
                    dve.bn_aggr(v_mv[:, 1, :], v_stat[:, 1, :, :]).then_inc(v_var, 1)
                if n == 4:
                    dve.wait_ge(ab_in, 16 * 4)
                    for t in range(NT):
                        dve.wait_ge(v_rstd, t + 1)
                        last = st.done(dve.tensor_scalar(vn[:, t, :], vn[:, t, :], v_mv[:, t, 0:1], rstd[:, 16 + t:17 + t],
                                                         ALU.subtract, ALU.mult))
                    st.wait(last)
                    st.link(dve.tensor_tensor(vn[:, :, :], vn[:, :, :], vg[:, None, :].to_broadcast([P, NT, D]), ALU.mult))
                    dve.tensor_tensor(vn[:, :, :], vn[:, :, :], vb[:, None, :].to_broadcast([P, NT, D]), ALU.add).then_inc(vn_ready, 1)
                if n == 8:
                    mixed(0)
                    mixed(1)
                if n == 9:
                    dve.wait_ge(yb_f, 1)
                    split_both(tmp[:, :, :], yTb_hi[:, :, :], yTb_lo[:, :, :], yb_ready)
                    mixed(2)
                if n == 10:
                    mixed(3)
                if n == 13:
                    gate_mul(0)
                if n == 15:
                    dve.wait_ge(col_ps, 4)
                    shift_and_scale(1, (0, 0)).then_inc(mod_ready, 1)

            def ffn(l, base):
                def conv(k, i, par):
                    for h in range(2):
                        dve.wait_ge(tap_done, val(22 * l + 2 * k + h + 1, i, 4))
                        for back in (1, 2):
                            for a in range(2):
                                col = 2 * FCH * l + FCH * h + 2 * k + a
                                o = cbuf[:, par, h, a * TOK + back:(a + 1) * TOK]
                                ins = dve.scalar_tensor_tensor(
                                    o, ps[:, 2 * par + h, a * TOK:(a + 1) * TOK - back],
                                    ffn_cols[:, 2 - back, bass.ds(val(col, i, 4), 1)], o, ALU.mult, ALU.add)
                                if back == 1 or a == 0:
                                    last = st.done(ins)
                            if back == 1:
                                st.wait(last)
                        ins.then_inc(up_free, 1)

                def gated(k, i, par):
                    dve.wait_ge(silu_done, val(11 * l + k + 1, i, 2))
                    dve.wait_ge(up_free, val(26 * l + 4 + 2 * k + 2, i, 4))
                    dve.wait_ge(tile_used, val(base + 3 * k - 1, i, 6))
                    st.link(dve.tensor_tensor(cbuf[:, par, 1, :], cbuf[:, par, 0, :], cbuf[:, par, 1, :], ALU.mult))
                    s = cbuf[:, par, 1, :].rearrange("p (a t) -> p a t", a=2)
                    st.link(dve.tensor_copy(yTa_hi[:, 2 * par:2 * par + 2, :], s))
                    dve.tensor_tensor(yTa_lo[:, 2 * par:2 * par + 2, :], s,
                                      yTa_hi[:, 2 * par:2 * par + 2, :].bitcast(F32), ALU.subtract).then_inc(aT_ready, 1)

                def loop_ada(i, r, j):
                    k = cact[:, bass.ds(i, 1)]
                    if l == 0:
                        a = ADA_FF + 2 * r + j
                        dve.wait_ge(ada_in[j], val(16 * (a // 2 + 1), i, 32))
                        ada_add(acc_of[LOOP_V[2 * r + j]], ada[:, j, :], k, val(2 * PRO + a, i, 4))
                    elif r == 0 and j == 0:
                        dve.wait_ge(ada_in[1], val(16 * (ADA_FF1 // 2 + 1), i, 16))
                        ada_add(acc_of[11], ada[:, 1, :], k, val(2 * PRO + ADA_FF1, i, 1))

                dve.sem_inc(up_free, 4)
                dve.sem_inc(aT_ready, 2)
                with dve.Fori(0, 5) as i:
                    st.enter(i, 2 * 8)
                    for r in range(2):
                        split_lo(base + 2 + 3 * r, i)
                        loop_ada(i, r, 0)
                        conv(r, i, r)
                        split_lo(base + 3 + 3 * r, i)
                        loop_ada(i, r, 1)
                        gated(r, i, r)
                        split_lo(base + 4 + 3 * r, i)
                    st.leave(5)
                split_lo(base + 32)
                conv(10, None, 0)
                gated(10, None, 0)
                gate_mul(2 * l + 1)
                if l == 0:
                    split_lo(base + 33)
                    split_lo(base + 34)

            residual(0)
            norm(1)
            split_h(1)
            ada_tiles(LATE0)
            for v in (9, 10):
                dve.wait_ge(bias_in[v], 16)
            ffn(0, FF0)
            dve.wait_ge(col_ps, 6)
            shift_and_scale(2, (0, 0)).then_inc(mod_ready, 1)
            residual(1)
            norm(2)
            split_h(2)
            split_lo(CD0 + 2)

            a_next[0] = ADA_MID

            def rotate(z):
                dve.wait_ge(qkv_s, z + 1)
                if z == 0:
                    dve.wait_ge(trig_ready, 1)
                else:
                    dve.wait_ge(rot_done, 1)
                v = qk[:, z, :, :].rearrange("p t (h d) -> p t h d", h=HEADS)
                x1, x2 = v[:, :, :, 0:HALF], v[:, :, :, HALF:ROT]
                sin = trig[:, 0, :, None, :].to_broadcast([P, NT, HEADS, HALF])
                cos = trig[:, 1, :, None, :].to_broadcast([P, NT, HEADS, HALF])
                t = [tmp[:, j, 0:P].rearrange("p (t h d) -> p t h d", t=NT, h=HEADS) for j in range(4)]
                for o, u, w in ((t[0], x1, cos), (t[1], x2, sin), (t[2], x2, cos), (t[3], x1, sin)):
                    last = st.done(dve.tensor_tensor(o, u, w, ALU.mult))
                st.wait(last)
                st.done(dve.tensor_tensor(x1, t[0], t[1], ALU.subtract))
                dve.tensor_tensor(x2, t[2], t[3], ALU.add).then_inc(rot_done, 1)

            def lowest(h):
                dve.wait_ge(score_ps, h + 1)
                if h == 0:
                    dve.wait_ge(mask_ready, 2)
                if h >= 2:
                    dve.wait_ge(probT_ps, h - 1)
                st.link(dve.scalar_tensor_tensor(prob[:, h % 2, :], ps[:, 4 + h % 2, 0:3 * P], -float(HD) ** -0.5, mask[:, :],
                                                 ALU.mult, ALU.add))
                for q in range(NT):
                    ins = dve.tensor_reduce(s_min[:, h % 2, q:q + 1], prob[:, h % 2, (0, P)[q]:(P, 3 * P)[q]], AX_X, ALU.min)
                    if q == 0:
                        st.done(ins)
                ins.then_inc(min_ready, 1)

            def normalise(h):
                dve.wait_ge(exp_done, h + 1)
                st.link(dve.reciprocal(s_sum[:, h % 2, :], s_sum[:, h % 2, :]))
                for q in range(NT):
                    s = prob[:, h % 2, (0, P)[q]:(P, 3 * P)[q]]
                    ins = dve.tensor_scalar(s, s, s_sum[:, h % 2, q:q + 1], None, ALU.mult)
                    if q == 0:
                        st.done(ins)
                ins.then_inc(prob_ready, 1)

            def softmax(h):
                lowest(h)
                lowest(h + 1)
                normalise(h)
                normalise(h + 1)

            def heads_out(j):
                dve.wait_ge(pv_ps, 2 * j + 2)
                split_both(ps[:, 1, TOK * (j % 2):TOK * (j % 2) + TOK], yTa_hi[:, 4 + j, :], yTa_lo[:, 4 + j, :], yd_ready)

            def gated_input(j):
                dve.wait_ge(ccs_ready, j + 1)
                dve.wait_ge(tile_used, CD0 + 8 + 3 * j)
                if j:
                    dve.wait_ge(yc_ready, j)
                dve.tensor_tensor(cm[:, :, :].rearrange("p a t -> p (a t)"), ccs[:, :, :].rearrange("p a t -> p (a t)"),
                                  ps[:, 3, :], ALU.mult).then_inc(cm_ready, 1)

            def gated_conv(j):
                dve.wait_ge(ctap_done, j + 1)
                for back in (1, 2):
                    for a in range(2):
                        col = R_CONV + 4 * (2 - back) + 2 * j + a
                        last = st.done(dve.scalar_tensor_tensor(cy[:, a, back:TOK], cm[:, a, 0:TOK - back], cols[:, col:col + 1],
                                                                cy[:, a, back:TOK], ALU.mult, ALU.add))
                    st.wait(last)
                dve.wait_ge(tile_used, CD0 + 9 + 3 * j)
                f = cy[:, :, :].rearrange("p a t -> p (a t)")
                st.link(dve.tensor_tensor(f, f, ps[:, 0, :], ALU.mult))
                split_both(cy[:, :, :], yTa_hi[:, 2 * j:2 * j + 2, :], yTa_lo[:, 2 * j:2 * j + 2, :], yc_ready)

            for n in range(16):
                if n < 15:
                    split_lo(CD0 + n + RING)
                    ada_tiles(ADA_CD.get(CD0 + n + RING, 0))
                if n in (1, 3):
                    rotate(n // 2)
                if n == 7:
                    gated_input(0)
                    softmax(0)
                if n == 8:
                    gated_conv(0)
                    softmax(2)
                if n == 9:
                    heads_out(0)
                    softmax(4)
                if n == 10:
                    gated_input(1)
                    heads_out(1)
                    softmax(6)
                if n == 11:
                    gated_conv(1)
                    heads_out(2)
                if n == 12:
                    heads_out(3)
                if n == 14:
                    gate_mul(2)
                    dve.wait_ge(col_ps, 8)
                    shift_and_scale(3, (0, 0)).then_inc(mod_ready, 1)
            residual(2)
            norm(3)
            split_h(3)
            ada_tiles(LATE1)
            ffn(1, FF1)
            residual(3)


_INS = ["x", "c", "positions", "ab_w_in", "ab_vnorm_g", "ab_vnorm_b", "ab_spatial_w", "ab_spatial_b", "ab_pool_w",
        "ab_pool_scale", "ab_w_out", "cd_w_in", "cd_conv_w", "cd_w_out", "ffn_w_up", "ffn_conv_w", "ffn_w_down",
        "ada_w", "ada_b", "norm_g"]


def kernel(**inputs):
    import concourse.bacc as bacc
    from concourse.bass_utils import run_bass_kernel_spmd

    nc = bacc.Bacc("TRN2", target_bir_lowering=False, num_devices=1)
    arrays, args = {}, []
    for name in _INS:
        a = np.ascontiguousarray(inputs[name])
        arrays[f"in_{name}"] = a
        args.append(nc.dram_tensor(f"in_{name}", a.shape, mybir.dt.from_np(a.dtype), kind="ExternalInput").ap())
    out = nc.dram_tensor("out", (1, TOK, D), F32, kind="ExternalOutput").ap()
    trunk(nc, *args, out)
    r = run_bass_kernel_spmd(nc, [arrays], core_ids=[0])
    return r.results[0]["out"]
```

```python
from contextlib import ExitStack

import numpy as np

import concourse.bass as bass
from concourse import mybir

F32 = mybir.dt.float32
F32R = mybir.dt.float32r
BF16 = mybir.dt.bfloat16
I32 = mybir.dt.int32
ALU = mybir.AluOpType
ACT = mybir.ActivationFunctionType
AX_X = mybir.AxisListType.X

P = 128
TOK = 256
NT = TOK // P
D = 1024
KD = D // P
A_GROUPS = 8
A_WIDTH = 1024
WINDOWS = (2, 4, 8, 16)
NB = len(WINDOWS)
PAD = max(WINDOWS)
C_WIDTH = 512
HEADS = 8
HD = 64
ROT = HD // 4
HALF = ROT // 2
FF = 2816
FCH = FF // P
STEPS = FCH // 2
EPS = 1e-6
BIG = 1e30

TILE = 2048
RAW = 6
RING = 3
LO_DVE = 768
PRO = 8
AB0, FF0, CD0, FF1, END = 0, 16, 49, 65, 98

R_NORM, R_POOL, R_CONV, R_ALL = 0, 64, 68, 80

LOOP_K = 5
REST = range(LOOP_K, KD)
ADA_TILES = [(v, k) for v in (2, 3, 4) for k in range(KD)] + [(v, k) for v in (6, 7) for k in REST]
ADA_AB = {3: 1, 4: 1, 6: 2, 7: 2, 8: 2, 9: 2, 10: 2, 11: 2, 12: 3, 13: 3, 14: 3, 15: 1}
LEAD = 1
LATE0 = 6
ADA_FF = len(ADA_TILES)
LOOP_V = (6, 7, 9, 10)
LOOP_ADDS = len(LOOP_V) + 1
ADA_TILES += [(v, k) for k in range(LOOP_K) for v in LOOP_V]
ADA_MID = len(ADA_TILES)
ADA_TILES += [(5, k) for k in REST]
TAIL0 = len(REST)
ADA_TILES += [(v, k) for v in (9, 10) for k in REST] + [(8, k) for k in range(KD)]
ADA_CD = {CD0 + 3: 2, CD0 + 4: 2, CD0 + 5: 2, CD0 + 6: 2, CD0 + 7: 2, CD0 + 8: 2, CD0 + 9: 2}
ADA_TILES += [(11, k) for k in REST]
LATE1 = len(REST)
ADA_FF1 = len(ADA_TILES)

Y_PAIRS = ((0, 1), (2, 3), (4, 5), (8, 9), (10, 11), (6, 7))


def added(a):
    return 2 * PRO + a + (LOOP_K if a >= ADA_MID else 0)


def ada_slot(a):
    if a < ADA_FF:
        return a % 3, a // 3
    b = a - ADA_MID
    return b % 3, ADA_FF // 3 + (2 * LOOP_K, 2 * LOOP_K, LOOP_K)[b % 3] + b // 3


def ada_freed(a):
    return added(a) - (1 if ADA_MID <= a < ADA_MID + 2 else 2)


def val(const, i=None, per=0):
    return const if i is None else i * per + const


WARM_ADA, WARM_H, WARM_X, WARM_T0, WARM_T1 = 2, 6, 11, 4, 2


class Steps:

    def __init__(self, eng, sem):
        self.eng, self.sem, self.n, self.i, self.per = eng, sem, 0, None, 0

    def done(self, ins):
        ins.then_inc(self.sem, 1)
        self.n += 1
        return val(self.n, self.i, self.per)

    def wait(self, value):
        self.eng.wait_ge(self.sem, value)

    def link(self, ins):
        self.wait(self.done(ins))

    def enter(self, i, per):
        self.first, self.i, self.per = self.n, i, per

    def leave(self, turns):
        assert self.n - self.first == self.per, (self.n - self.first, self.per)
        self.n, self.i = self.first + turns * self.per, None


def trunk(nc, x, c, positions, ab_w_in, ab_vnorm_g, ab_vnorm_b, ab_spatial_w, ab_spatial_b,
          ab_pool_w, ab_pool_scale, ab_w_out, cd_w_in, cd_conv_w, cd_w_out, ffn_w_up, ffn_conv_w,
          ffn_w_down, ada_w, ada_b, norm_g, out):
    with ExitStack() as ctx:
        def sb(name, shape, dt=F32):
            return ctx.enter_context(nc.sbuf_tensor(name, shape, dt))

        def sem(name):
            return ctx.enter_context(nc.semaphore(name))

        def overlay(name, size, *groups):
            made = []
            for group in groups:
                with ExitStack() as inner:
                    made += [inner.enter_context(nc.sbuf_tensor(*t)) for t in group]
            sb(name, [P, size])
            return made

        raw = sb("raw", [P, RAW, TILE])
        w_hi = sb("w_hi", [P, RING, TILE], F32R)
        w_lo = sb("w_lo", [P, RING, TILE], F32R)
        ada = sb("ada", [P, 3, D])
        xs = sb("xs", [P, NT, D])
        hT_hi = sb("hT_hi", [P, KD, TOK], F32R)
        hT_lo = sb("hT_lo", [P, KD, TOK], F32R)
        gate = sb("gate", [P, D])
        acc = sb("acc", [P, 3, D])
        tmp = sb("tmp", [P, 4, TOK])
        ident = sb("ident", [P, P])
        ones = sb("ones", [P, 1])
        cols = sb("cols", [P, R_ALL])
        ffn_cols = sb("ffn_cols", [P, 3, 2 * 2 * FCH])
        mod = sb("mod", [P, 4, 2, KD])
        cact = sb("cact", [P, KD])
        zero = sb("zero", [P, P], BF16)
        sums = sb("sums", [P, 16])
        rstd = sb("rstd", [P, 18])
        nhalf = sb("nhalf", [P, 2])
        cnt_i = sb("cnt_i", [P, PAD], I32)
        cnt_f = sb("cnt_f", [P, PAD])
        inv_cnt = sb("inv_cnt", [P, NB, PAD])
        pos_i = sb("pos_i", [P, NT], I32)
        pos_f = sb("pos_f", [P, NT])
        inv_freq = sb("inv_freq", [P, HALF])
        angle = sb("angle", [P, NT * HALF])
        turns_i = sb("turns_i", [P, 2, NT * HALF], I32)
        turns_f = sb("turns_f", [P, 2, NT * HALF])
        trig = sb("trig", [P, 2, NT, HALF])
        v_stat = sb("v_stat", [P, NT, 2, 6])
        v_mv = sb("v_mv", [P, NT, 2])
        s_min = sb("s_min", [P, 2, 2])
        s_sum = sb("s_sum", [P, 2, 2])
        ws_raw, small_rows, conv_rows, c_rows, pool_x, pool_a, pool_b, yTa_hi, yTa_lo = overlay(
            "place_y", 16 * TOK,
            [("ws_raw", [P, A_GROUPS, P], F32), ("small_rows", [R_ALL, P], F32), ("conv_rows", [4 * FCH, 3, P], F32),
             ("c_rows", [KD, P], F32)],
            [("pool_x", [P, NB, PAD + TOK], F32), ("pool_a", [P, NB, PAD + TOK], F32), ("pool_b", [P, NB - 1, PAD + TOK], F32)],
            [("yTa_hi", [P, KD, TOK], F32R), ("yTa_lo", [P, KD, TOK], F32R)])
        vg, vb, yTb_hi, yTb_lo, ccs, cm, cy = overlay(
            "place_b", 8 * TOK,
            [("vg", [P, D], F32), ("vb", [P, D], F32)],
            [("yTb_hi", [P, NB, TOK], F32R), ("yTb_lo", [P, NB, TOK], F32R)],
            [("ccs", [P, 2, TOK], F32), ("cm", [P, 2, TOK], F32), ("cy", [P, 2, TOK], F32)])
        xh, vn, cbuf, qk = overlay(
            "place_x", NT * D,
            [("xh", [P, NT, D], F32)], [("vn", [P, NT, A_WIDTH], F32)],
            [("cbuf", [P, 2, 2, 2 * TOK], F32)], [("qk", [P, 2, NT, HEADS * HD], F32)])
        bs, wsT, pool_w, gu, mx, accs, vs, qT, kT, prob, probT, mask = overlay(
            "place_m", 20 * TOK,
            [("bs", [P, A_GROUPS, P], F32),
             ("wsT", [P, A_GROUPS, P], F32), ("pool_w", [P, NB, P], F32),
             ("gu", [P, 2, 2 * TOK], F32), ("mx", [P, 2 * TOK], F32)],
            [("accs", [P, 2, D], F32)],
            [("vs", [P, NT, HEADS * HD], F32), ("qT", [P, 4, TOK], F32), ("kT", [P, 4, TOK], F32),
             ("prob", [P, 2, 3 * P], F32), ("probT", [P, 2, 3 * P], F32), ("mask", [P, 3 * P], F32)])
        ps = ctx.enter_context(nc.psum_tensor("ps", [P, 8, 512], F32))

        raw_in = [sem(f"raw_in{i}") for i in range(RAW)]
        ada_in = [sem(f"ada_in{i}") for i in range(3)]
        x_in = sem("x_in")
        c_in = sem("c_in")
        acc_zero = sem("acc_zero")
        pos_in = sem("pos_in")
        rows_in = sem("rows_in")
        bias_in = [sem(f"bias_in{v}") for v in range(12)]
        ws_in = sem("ws_in")
        ab_in = sem("ab_in")
        grow_in = sem("grow_in")
        out_done = sem("out_done")
        hi_done = sem("hi_done")
        lo_dve = sem("lo_dve")
        lo_pool = sem("lo_pool")
        tile_used = sem("tile_used")
        ada_step = sem("ada_step")
        dve_step = sem("dve_step")
        pool_step = sem("pool_step")
        consts_ready = sem("consts_ready")
        cT_ps = sem("cT_ps")
        rowsT_ps = sem("rowsT_ps")
        wsT_ps = sem("wsT_ps")
        ws_masked = sem("ws_masked")
        small_ready = sem("small_ready")
        wsT_ready = sem("wsT_ready")
        cact_ready = sem("cact_ready")
        angles_ready = sem("angles_ready")
        trig_ready = sem("trig_ready")
        col_ps = sem("col_ps")
        mod_ready = sem("mod_ready")
        gate_ps = sem("gate_ps")
        gate_ready = sem("gate_ready")
        sq_done = sem("sq_done")
        rs_done = sem("rs_done")
        xh_done = sem("xh_done")
        xT_ps = sem("xT_ps")
        hf_done = sem("hf_done")
        h_done = sem("h_done")
        x_ready = sem("x_ready")
        y_ps = sem("y_ps")
        v_ready = sem("v_ready")
        v_var = sem("v_var")
        v_rstd = sem("v_rstd")
        vn_ready = sem("vn_ready")
        px_ready = sem("px_ready")
        window_sums = sem("window_sums")
        pooled = sem("pooled")
        poolmix_ps = sem("poolmix_ps")
        yb_f = sem("yb_f")
        gu_ready = sem("gu_ready")
        mix_ps = sem("mix_ps")
        y_ready = sem("y_ready")
        yb_ready = sem("yb_ready")
        up_free = sem("up_free")
        tap_done = sem("tap_done")
        silu_done = sem("silu_done")
        aT_ready = sem("aT_ready")
        qkv_s = sem("qkv_s")
        rot_done = sem("rot_done")
        qkT_ps = sem("qkT_ps")
        qkT_ready = sem("qkT_ready")
        ccs_ready = sem("ccs_ready")
        cm_ready = sem("cm_ready")
        ctap_done = sem("ctap_done")
        yc_ready = sem("yc_ready")
        mask_ready = sem("mask_ready")
        score_ps = sem("score_ps")
        min_ready = sem("min_ready")
        exp_done = sem("exp_done")
        prob_ready = sem("prob_ready")
        probT_ps = sem("probT_ps")
        probT_ready = sem("probT_ready")
        pv_ps = sem("pv_ps")
        yd_ready = sem("yd_ready")

        ab_in_w = ab_w_in[0].rearrange("(k p) n -> p k n", p=P)
        ab_out_w = ab_w_out[0].rearrange("(k p) n -> p k n", p=P)
        cd_in_w = cd_w_in[0].rearrange("(k p) n -> p k n", p=P)
        cd_out_w = cd_w_out[0].rearrange("(k p) n -> p k n", p=P)
        up_w = [ffn_w_up[l].rearrange("(k p) n -> p k n", p=P) for l in range(2)]
        down_w = [ffn_w_down[l].rearrange("(k p) n -> p k n", p=P) for l in range(2)]
        ada_v = [ada_w[l].rearrange("(k p) n -> p k n", p=P) for l in range(2)]
        x_v = x[0].rearrange("(t p) d -> p t d", p=P)
        out_v = out[0].rearrange("(t p) d -> p t d", p=P)

        def mixer_tile(n):
            if n < FF0:
                if n < 4:
                    return ab_in_w[:, 4 * (n % 2):4 * (n % 2) + 4, A_WIDTH + 512 * (n // 2):A_WIDTH + 512 * (n // 2) + 512]
                if n < 6:
                    return ab_in_w[:, :, 2 * A_WIDTH + 256 * (n - 4):2 * A_WIDTH + 256 * (n - 3)]
                if n < 10:
                    return ab_in_w[:, :, 256 * (n - 6):256 * (n - 5)]
                k = Y_PAIRS[n - 10][0]
                return ab_out_w[:, k:k + 2, :]
            n -= CD0
            if n < 6:
                c0 = 3 * C_WIDTH + 512 * (n // 2)
                return cd_in_w[:, 4 * (n % 2):4 * (n % 2) + 4, c0:c0 + 512]
            if n < 12:
                c0 = (C_WIDTH, 2 * C_WIDTH, 0)[n % 3] + 256 * ((n - 6) // 3)
                return cd_in_w[:, :, c0:c0 + 256]
            return cd_out_w[:, 2 * (n - 12):2 * (n - 12) + 2, :]

        def as_k4(w, slot):
            return w[:, slot, :].rearrange("p (k n) -> p k n", k=4)

        def as_k8(w, slot):
            return w[:, slot, :].rearrange("p (k n) -> p k n", k=8)

        def as_k2(w, slot):
            return w[:, slot, :].rearrange("p (k n) -> p k n", k=2)

        def y_of(t):
            return ps[:, 4 + 2 * t:6 + 2 * t, :].rearrange("p b n -> p (b n)")

        acc_of = {v: acc[:, slot, :] for v, slot in
                  {0: 0, 1: 1, 2: 2, 3: 0, 4: 1, 5: 2, 9: 0, 10: 1, 8: 2, 11: 2}.items()}
        acc_of.update({6: accs[:, 0, :], 7: accs[:, 1, :]})

        def h_room(b):
            if b < 2:
                return tmp[:, 2 * b:2 * b + 2, :]
            return gate[:, (b - 2) * 2 * TOK:(b - 1) * 2 * TOK].rearrange("p (a t) -> p a t", a=2)

        block = ctx.enter_context(nc.Block())

        @block.sync
        def _(sp):
            def weights(n, i, src, k):
                m = n + PRO
                if n >= RAW:
                    sp.wait_ge(lo_dve, val(n - RAW + 1, i, 6))
                    sp.wait_ge(lo_pool, val(n - RAW + 1, i, 6))
                elif m >= RAW:
                    sp.wait_ge(ada_step, 2 * (m - RAW) + 2)
                dst = raw[:, m % RAW, :].rearrange("p (k n) -> p k n", k=k)
                sp.dma_start(dst, src).then_inc(raw_in[m % RAW], 16)

            def ada_src(v, k):
                return ada_v[v // 6][:, k, (v % 6) * D:(v % 6 + 1) * D]

            def ada_tile(a, src):
                if a >= 3:
                    sp.wait_ge(ada_step, ada_freed(a))
                slot, _ = ada_slot(a)
                sp.dma_start(ada[:, slot, :], src).then_inc(ada_in[slot], 16)

            a_next = [0]

            def ada_tiles(count):
                for _ in range(count):
                    ada_tile(a_next[0], ada_src(*ADA_TILES[a_next[0]]))
                    a_next[0] += 1

            def straight(first, last, table):
                for n in range(first, last):
                    src = mixer_tile(n)
                    weights(n, None, src, src.shape[1])
                    ada_tiles(table.get(n - LEAD, 0))

            def first_ada(m):
                if m >= RAW:
                    sp.wait_ge(ada_step, 2 * (m - RAW) + 2)
                v, k = m // 4, 2 * (m % 4)
                sp.dma_start(raw[:, m % RAW, :].rearrange("p (k n) -> p k n", k=2),
                             ada_v[0][:, k:k + 2, v * D:(v + 1) * D]).then_inc(raw_in[m % RAW], 16)

            def bias(v):
                sp.wait_ge(acc_zero, v + 1)
                sp.dma_start(acc_of[v][0:1, :], ada_b[0:1, v * D:(v + 1) * D]).then_inc(bias_in[v], 16)

            sp.dma_start(c_rows[:, :], c.rearrange("o (k p) -> (o k) p", p=P)).then_inc(c_in, 16)
            first_ada(0)
            bias(0)
            sp.dma_start(small_rows[R_NORM:R_POOL, :], norm_g.rearrange("l n (k p) -> (l n k) p", p=P)).then_inc(rows_in, 16)
            first_ada(1)
            bias(1)
            bias(2)
            first_ada(2)
            sp.dma_start(small_rows[R_POOL:R_CONV, :], ab_pool_scale.rearrange("o (k p) -> (o k) p", p=P)).then_inc(rows_in, 16)
            sp.dma_start(small_rows[R_CONV:R_ALL, :], cd_conv_w.rearrange("o t (k p) -> (o t k) p", p=P)).then_inc(rows_in, 16)
            for l in range(2):
                sp.dma_start(conv_rows[2 * FCH * l:2 * FCH * (l + 1), :, :],
                             ffn_conv_w[l].rearrange("t (k p) -> k t p", p=P)).then_inc(rows_in, 16)
            first_ada(3)
            sp.dma_start(xs[:, :, :], x_v).then_inc(x_in, 16)
            for m in range(4, PRO):
                first_ada(m)
            sp.dma_start(pos_i[:, :], positions.rearrange("o (t p) -> p (o t)", p=P),
                         allow_slow_non_contiguous=True).then_inc(pos_in, 16)
            sp.dma_start(ws_raw[:, :, :], ab_spatial_w[0].rearrange("g i j -> i g j")).then_inc(ws_in, 16)
            straight(AB0, 4, ADA_AB)
            for t, src in ((vg, ab_vnorm_g[0]), (vb, ab_vnorm_b[0])):
                sp.dma_start(t[:, :], src.partition_broadcast(P)).then_inc(ab_in, 16)
            sp.dma_start(bs[:, :, :].rearrange("p g i -> p (g i)"),
                         ab_spatial_b[0].rearrange("g i -> (g i)").partition_broadcast(P)).then_inc(ab_in, 16)
            sp.dma_start(pool_w[:, :, :], ab_pool_w[0].rearrange("g d e -> d g e")).then_inc(ab_in, 16)
            straight(4, 10, ADA_AB)
            sp.wait_ge(h_done, 4)
            sp.dma_start(gate[:, :], norm_g[0, 1].partition_broadcast(P)).then_inc(grow_in, 16)
            straight(10, FF0, ADA_AB)

            def ffn(l, base):
                table = (ADA_AB, {})[l]

                def up(s_col, n, i):
                    weights(n, i, up_w[l][:, :, s_col], KD)

                def step_weights(c, i, first):
                    up(bass.ds(val(256 * first, i, 512), 256), c, i)
                    up(bass.ds(val(FF + 256 * first, i, 512), 256), c + 1, i)
                    weights(c + 2, i, down_w[l][:, bass.ds(val(2 * first - 2, i, 4), 2), :], 2)

                def loop_ada(i, r, k):
                    def src(v):
                        return ada_v[1 if v > 5 else 0][:, k, (v % 6) * D:(v % 6 + 1) * D].rearrange("p o n -> p (o n)")
                    if l == 0:
                        first = added(ADA_FF)
                        for j in range(2):
                            sp.wait_ge(ada_step, val(first - 1 + 2 * r + j, i, LOOP_ADDS))
                            sp.dma_start(ada[:, j, :], src(LOOP_V[2 * r + j])).then_inc(ada_in[j], 16)
                        if r == 0:
                            sp.wait_ge(ada_step, val(first, i, LOOP_ADDS))
                            sp.dma_start(ada[:, 2, :], src(5)).then_inc(ada_in[2], 16)
                    elif r == 0:
                        sp.wait_ge(ada_step, val(added(ADA_FF1), i, 1))
                        sp.dma_start(ada[:, 2, :], src(11)).then_inc(ada_in[2], 16)

                up(slice(0, 256), base, None)
                ada_tiles(table.get(base - LEAD, 0))
                up(slice(FF, FF + 256), base + 1, None)
                ada_tiles(table.get(base + 1 - LEAD, 0))
                step_weights(base + 2, None, 1)
                ada_tiles((LATE0, LATE1)[l])
                with sp.Fori(0, 4) as i:
                    for r in range(2):
                        loop_ada(i, r, bass.ds(i, 1))
                        step_weights(base + 5 + 3 * r, i, 2 + r)
                if l == 0:
                    a_next[0] = ADA_MID
                last_k = slice(LOOP_K - 1, LOOP_K)
                loop_ada(LOOP_K - 1, 0, last_k)
                step_weights(base + 29, None, STEPS - 1)
                loop_ada(LOOP_K - 1, 1, last_k)
                weights(base + 32, None, down_w[l][:, 2 * STEPS - 2:2 * STEPS, :], 2)
                if l == 0:
                    ada_tiles(TAIL0)
                    weights(CD0, None, mixer_tile(CD0), 4)
                    weights(CD0 + 1, None, mixer_tile(CD0 + 1), 4)

            ffn(0, FF0)
            straight(CD0 + 2, FF1, ADA_CD)
            ffn(1, FF1)
            for t in range(NT):
                sp.wait_ge(x_ready, 2 * 3 + t + 1)
                sp.dma_start(out_v[:, t, :], xs[:, t, :]).then_inc(out_done, 16)
            sp.wait_ge(out_done, 16 * NT)

        @block.gpsimd
        def _(pool):
            st = Steps(pool, pool_step)

            def split_lo(n, i=None):
                pool.wait_ge(hi_done, val(n + 1, i, 6))
                pool.tensor_tensor(w_lo[:, n % RING, LO_DVE:TILE], raw[:, (n + PRO) % RAW, LO_DVE:TILE],
                                   w_hi[:, n % RING, LO_DVE:TILE].bitcast(F32), ALU.subtract).then_inc(lo_pool, 1)

            def inv_rms(src, dst, scale):
                st.link(pool.tensor_scalar(dst, src, scale, EPS, ALU.mult, ALU.add))
                return pool.tensor_tensor(dst, dst, nhalf[:, 0:1], ALU.pow)

            def boundary(r):
                for t in range(NT):
                    pool.wait_ge(sq_done, 4 * r + t + 3)
                    j = 4 * r + t + 2
                    inv_rms(sums[:, j:j + 1], rstd[:, j:j + 1], 1.0 / D).then_inc(rs_done, 1)
                if r < 3:
                    norm(r + 1)
                    split_lo((FF0, CD0, FF1)[r] + 1)

            def norm(m):
                for t in range(NT):
                    pool.wait_ge(sq_done, 4 * m + t + 1)
                    j = 4 * m + t
                    inv_rms(sums[:, j:j + 1], rstd[:, j:j + 1], 1.0 / D).then_inc(rs_done, 1)

            def start_acc(*vs):
                for v in vs:
                    last = st.done(pool.memset(acc_of[v], 0.0))
                for v in vs:
                    st.wait(last)
                    pool.dma_start(acc_of[v][0:1, :], ada_b[v // 6:v // 6 + 1, (v % 6) * D:(v % 6 + 1) * D]).then_inc(bias_in[v], 16)

            st.link(pool.memset(ident[:, :], 0.0))
            pool.affine_select(out=ident[:, :], in_=ident[:, :], compare_op=ALU.not_equal, fill=1.0, base=0,
                               pattern=[[-1, P]], channel_multiplier=1).then_inc(consts_ready, 1)
            pool.memset(ones[:, :], 1.0).then_inc(consts_ready, 1)
            pool.memset(zero[:, :], 0.0).then_inc(consts_ready, 1)
            st.link(pool.memset(nhalf[:, :], -0.5))
            freq = np.float32(500000.0) ** (-np.arange(0, ROT, 2, dtype=np.float32) / np.float32(ROT))
            for j in range(HALF):
                pool.memset(inv_freq[:, j:j + 1], float(freq[j])).then_inc(consts_ready, 1)
            pool.iota(cnt_i[:, :], pattern=[[1, PAD]], base=1, channel_multiplier=0).then_inc(consts_ready, 1)
            norm(0)
            pool.wait_ge(ws_in, 16)
            pool.affine_select(out=ws_raw[:, :, :], in_=ws_raw[:, :, :], compare_op=ALU.is_ge, fill=0.0, base=0,
                               pattern=[[0, A_GROUPS], [-1, P]], channel_multiplier=1).then_inc(ws_masked, 1)
            for n in range(3):
                split_lo(n)
            pool.wait_ge(col_ps, 2)
            start_acc(3, 4)
            for n in range(3, 6):
                split_lo(n)
            pool.wait_ge(v_var, 1)
            for t in range(NT):
                inv_rms(v_mv[:, t, 1:2], rstd[:, 16 + t:17 + t], 1.0).then_inc(v_rstd, 1)
            split_lo(6)
            split_lo(7)
            split_lo(8)
            pool.wait_ge(px_ready, 3)
            W = PAD + TOK
            st.link(pool.tensor_tensor(pool_a[:, :, 1:W], pool_x[:, :, 1:W], pool_x[:, :, 0:W - 1], ALU.add))
            st.link(pool.tensor_tensor(pool_b[:, :, 3:W], pool_a[:, 1:4, 3:W], pool_a[:, 1:4, 1:W - 2], ALU.add))
            st.link(pool.tensor_tensor(pool_a[:, 2:4, 7:W], pool_b[:, 1:3, 7:W], pool_b[:, 1:3, 3:W - 4], ALU.add))
            pool.tensor_tensor(pool_b[:, 2:3, 15:W], pool_a[:, 3:4, 15:W], pool_a[:, 3:4, 7:W - 8], ALU.add).then_inc(window_sums, 1)
            split_lo(9)
            for n in range(10, FF0 + 1):
                split_lo(n)
                if n == 14:
                    pool.wait_ge(gate_ps, 1)
                    start_acc(5)
                    pool.wait_ge(y_ready, 4)
                    start_acc(6, 7)
            boundary(0)
            pool.wait_ge(col_ps, 4)
            start_acc(9, 10)

            def ffn(l, base):
                with pool.Fori(0, 5) as i:
                    for c in range(6):
                        split_lo(base + 2 + c, i)
                split_lo(base + 32)
                if l == 0:
                    split_lo(base + 33)

            ffn(0, FF0)
            boundary(1)
            pool.wait_ge(gate_ps, 2)
            start_acc(8)
            pool.wait_ge(col_ps, 6)
            st.link(pool.memset(mask[:, :], 0.0))
            for b in (0, 2):
                m = mask[:, b * P:(b + 1) * P]
                pool.affine_select(out=m, in_=m, compare_op=ALU.is_ge, fill=BIG, base=0, pattern=[[-1, P]],
                                   channel_multiplier=1).then_inc(mask_ready, 1)
            for n in range(CD0 + 2, FF1 + 1):
                split_lo(n)
            boundary(2)
            pool.wait_ge(gate_ps, 3)
            start_acc(11)
            ffn(1, FF1)
            boundary(3)

        @block.scalar
        def _(act):
            def split_hi(n, i=None):
                m = n + PRO
                act.wait_ge(raw_in[m % RAW], val(16 * (m // RAW + 1), i, 16))
                if n >= RING:
                    act.wait_ge(tile_used, val(n - RING + 1, i, 6))
                act.activation(w_hi[:, n % RING, :], raw[:, m % RAW, :], ACT.Copy).then_inc(hi_done, 1)

            def squares_of_x(m):
                for t in range(NT):
                    if m == 0:
                        act.wait_ge(x_in, 16)
                    else:
                        act.wait_ge(x_ready, 2 * (m - 1) + t + 1)
                    j = 4 * m + t
                    act.activation(xh[:, t, :], xs[:, t, :], ACT.Square,
                                   accum_out=sums[:, j:j + 1]).then_inc(sq_done, 1)

            def shift_scale(m):
                act.wait_ge(mod_ready, m + 1)
                for b in range(4):
                    act.wait_ge(xT_ps, 4 * m + b + 1)
                    for a in range(2):
                        k = 2 * b + a
                        ins = act.activation(h_room(b)[:, a, :], ps[:, b, a * TOK:(a + 1) * TOK], ACT.Identity,
                                             scale=mod[:, m, 1, k:k + 1], bias=mod[:, m, 0, k:k + 1])
                    ins.then_inc(hf_done, 1)

            def squares_of_y(r):
                for t in range(NT):
                    if t == 0:
                        act.wait_ge(y_ps, r + 1)
                    else:
                        act.wait_ge(tile_used, (FF0, CD0, FF1, END)[r])
                    j = 4 * r + t + 2
                    junk = hT_lo[:, 4 * t:4 * t + 4, :].rearrange("p k t -> p (k t)")
                    act.activation(junk, y_of(t), ACT.Square, accum_out=sums[:, j:j + 1]).then_inc(sq_done, 1)

            def gain_row(r):
                act.wait_ge(h_done, 4 * (r + 1))
                act.dma_start(gate[:, :], norm_g[r // 2, 1 + 2 * (r % 2)].partition_broadcast(P)).then_inc(grow_in, 16)

            act.wait_ge(cT_ps, 1)
            act.activation(cact[:, :], ps[:, 4, 0:KD], ACT.Silu).then_inc(cact_ready, 1)
            act.wait_ge(rowsT_ps, 1)
            act.activation(cols[:, :], ps[:, 0, 0:R_ALL], ACT.Copy).then_inc(small_ready, 1)
            act.activation(ffn_cols[:, :, :].rearrange("p t k -> p (t k)"), ps[:, 1, 0:12 * FCH], ACT.Copy).then_inc(small_ready, 1)
            squares_of_x(0)
            for t in range(NT):
                act.wait_ge(rs_done, t + 1)
                act.activation(xh[:, t, :], xs[:, t, :], ACT.Copy, scale=rstd[:, t:t + 1]).then_inc(xh_done, 1)
            split_hi(0)
            shift_scale(0)
            split_hi(1)
            act.wait_ge(wsT_ps, 1)
            act.activation(wsT[:, :, :].rearrange("p (b g) i -> p b (g i)", b=2), ps[:, 6:8, :], ACT.Copy).then_inc(wsT_ready, 1)
            split_hi(2)

            for n in range(AB0, FF0):
                if n < FF0 - 1 and n not in (1, 3):
                    split_hi(n + RING)
                if n == 2:
                    act.wait_ge(angles_ready, 1)
                    act.activation(trig[:, :, :, :].rearrange("p s t j -> p (s t j)"),
                                   turns_f[:, :, :].rearrange("p s j -> p (s j)"), ACT.Sin).then_inc(trig_ready, 1)
                if n == 1 or n == 3:
                    b = 4 + (n // 2) * 2
                    h = n // 2
                    act.wait_ge(tile_used, n + 1)
                    act.activation(vn[:, :, 512 * h:512 * h + 512], ps[:, b:b + 2, :], ACT.Gelu_apprx_tanh).then_inc(v_ready, 1)
                    split_hi(n + RING)
                if n in (4, 5):
                    act.wait_ge(tile_used, n + 1)
                    act.activation(pool_x[:, 2 * (n - 4):2 * (n - 4) + 2, PAD:PAD + TOK],
                                   ps[:, n - 4, :].rearrange("p (a t) -> p a t", a=2), ACT.Copy).then_inc(px_ready, 1)
                if 6 <= n < 10:
                    j = n - 6
                    act.wait_ge(tile_used, n + 1)
                    if j >= 2:
                        act.wait_ge(y_ready, j - 1)
                    act.activation(gu[:, j % 2, :], ps[:, (2, 0)[j % 2], :], ACT.Gelu_apprx_tanh).then_inc(gu_ready, 1)
                if n == 8:
                    act.wait_ge(poolmix_ps, 1)
                    for g in range(NB):
                        ins = act.activation(tmp[:, g, :], ps[:, 6 + g // 2, (g % 2) * TOK:(g % 2 + 1) * TOK], ACT.Copy,
                                             scale=cols[:, R_POOL + g:R_POOL + g + 1])
                    ins.then_inc(yb_f, 1)

            def ffn(l, base):
                W2 = 2

                def taps(k, i, par):
                    act.wait_ge(aT_ready, val(13 * l + k + 1, i, 2))
                    for h in range(2):
                        act.wait_ge(tile_used, val(base + 3 * k + h, i, 6))
                        for a in range(2):
                            col = 2 * FCH * l + FCH * h + 2 * k + a
                            ins = act.activation(cbuf[:, par, h, a * TOK:(a + 1) * TOK],
                                                 ps[:, 2 * par + h, a * TOK:(a + 1) * TOK], ACT.Copy,
                                                 scale=ffn_cols[:, W2, bass.ds(val(col, i, 4), 1)])
                        ins.then_inc(tap_done, 1)

                def silu(k, i, par):
                    act.wait_ge(up_free, val(26 * l + 4 + 2 * k + 1, i, 4))
                    act.activation(cbuf[:, par, 0, :], cbuf[:, par, 0, :], ACT.Silu).then_inc(silu_done, 1)

                def step(k, i, last=False):
                    taps(k, i, k % 2)
                    silu(k, i, k % 2)
                    split_hi(base + 4 + 3 * k, i)
                    split_hi(base + 5 + 3 * k, i)
                    if not last:
                        split_hi(base + 6 + 3 * k, i)

                split_hi(base + 2)
                gain_row(2 * l + 1)
                split_hi(base + 3)
                act.wait_ge(tile_used, base + 2)
                with act.Fori(0, 4) as i:
                    step(0, i)
                    step(1, i)
                step(8, None)
                step(9, None, last=True)
                taps(10, None, 0)
                silu(10, None, 0)
                if l == 0:
                    split_hi(base + 33)
                    split_hi(base + 34)

            squares_of_y(0)
            squares_of_x(1)
            shift_scale(1)
            ffn(0, FF0)
            squares_of_y(1)
            squares_of_x(2)
            shift_scale(2)
            split_hi(CD0 + 2)
            gain_row(2)

            def exps(h):
                act.wait_ge(min_ready, h + 1)
                for q in range(NT):
                    s = prob[:, h % 2, (0, P)[q]:(P, 3 * P)[q]]
                    ins = act.activation(s, s, ACT.Exp, scale=-1.0, bias=s_min[:, h % 2, q:q + 1],
                                         accum_out=s_sum[:, h % 2, q:q + 1])
                ins.then_inc(exp_done, 1)

            def move_probT(h):
                act.wait_ge(probT_ps, h + 1)
                if h >= 2:
                    act.wait_ge(pv_ps, h - 1)
                act.activation(probT[:, h % 2, :], ps[:, 6 + h % 2, 0:3 * P], ACT.Copy).then_inc(probT_ready, 1)

            def ctaps(j):
                act.wait_ge(cm_ready, j + 1)
                if j:
                    act.wait_ge(yc_ready, j)
                for a in range(2):
                    col = R_CONV + 4 * 2 + 2 * j + a
                    ins = act.activation(cy[:, a, :], cm[:, a, :], ACT.Copy, scale=cols[:, col:col + 1])
                ins.then_inc(ctap_done, 1)

            for n in range(16):
                if n < 15:
                    split_hi(CD0 + n + RING)
                used = CD0 + n + 1
                if n in (1, 3, 5):
                    act.wait_ge(tile_used, used)
                    b = (4, 6, 0)[n // 2]
                    dst = vs[:, :, :] if n == 5 else qk[:, n // 2, :, :]
                    act.activation(dst, ps[:, b:b + 2, :], ACT.Copy).then_inc(qkv_s, 1)
                if n == 6:
                    act.wait_ge(tile_used, used)
                    act.activation(ccs[:, :, :].rearrange("p a t -> p (a t)"), ps[:, 2, :], ACT.Copy).then_inc(ccs_ready, 1)
                    for z, dst in enumerate((qT, kT)):
                        act.wait_ge(qkT_ps, z + 1)
                        act.activation(dst[:, :, :].rearrange("p (b a) t -> p b (a t)", b=2), ps[:, 4 + 2 * z:6 + 2 * z, :],
                                       ACT.Copy).then_inc(qkT_ready, 1)
                if n == 7:
                    ctaps(0)
                    exps(0)
                    exps(1)
                if n == 8:
                    move_probT(0)
                    move_probT(1)
                    exps(2)
                    exps(3)
                if n == 9:
                    act.wait_ge(tile_used, used)
                    act.wait_ge(cm_ready, 1)
                    act.activation(ccs[:, :, :].rearrange("p a t -> p (a t)"), ps[:, 2, :], ACT.Copy).then_inc(ccs_ready, 1)
                    move_probT(2)
                    move_probT(3)
                    exps(4)
                    exps(5)
                if n == 10:
                    ctaps(1)
                    move_probT(4)
                    move_probT(5)
                    exps(6)
                    exps(7)
                if n == 11:
                    move_probT(6)
                    move_probT(7)
            squares_of_y(2)
            squares_of_x(3)
            shift_scale(3)
            ffn(1, FF1)
            squares_of_y(3)

        @block.tensor
        def _(pe):
            def need(n, i=None):
                pe.wait_ge(hi_done, val(n + 1, i, 6))
                pe.wait_ge(lo_dve, val(n + 1, i, 6))
                pe.wait_ge(lo_pool, val(n + 1, i, 6))

            def tile_T(n, bank, i=None):
                need(n, i)
                hi, lo = as_k8(w_hi, n % RING), as_k8(w_lo, n % RING)
                for a in range(2):
                    o = ps[:, bank, a * TOK:(a + 1) * TOK]
                    f = slice(a * P, (a + 1) * P)
                    for k in range(KD):
                        pe.matmul(o, hi[:, k, f], hT_hi[:, k, :], start=(k == 0), stop=False)
                        pe.matmul(o, hi[:, k, f], hT_lo[:, k, :], start=False, stop=False)
                        ins = pe.matmul(o, lo[:, k, f], hT_hi[:, k, :], start=False, stop=(k == KD - 1))
                ins.then_inc(tile_used, 1)

            def tile_M(n, bank):
                need(n)
                hi, lo = as_k4(w_hi, n % RING), as_k4(w_lo, n % RING)
                kh = (n - (CD0 if n >= CD0 else 0)) % 2
                for t in range(NT):
                    o = ps[:, bank + t, :]
                    f = slice(t * P, (t + 1) * P)
                    for k in range(4):
                        kk = 4 * kh + k
                        if n in (AB0, AB0 + 1, CD0, CD0 + 1) and t == 0 and k % 2 == 0:
                            pe.wait_ge(h_done, (0 if n < CD0 else 8) + kk // 2 + 1)
                        pe.matmul(o, hT_hi[:, kk, f], hi[:, k, :], start=(kk == 0), stop=False)
                        pe.matmul(o, hT_hi[:, kk, f], lo[:, k, :], start=False, stop=False)
                        ins = pe.matmul(o, hT_lo[:, kk, f], hi[:, k, :], start=False, stop=(kk == KD - 1))
                ins.then_inc(tile_used, 1)

            def tile_Y(n, y_hi, y_lo, first, last, i=None):
                need(n, i)
                hi, lo = as_k2(w_hi, n % RING), as_k2(w_lo, n % RING)
                for t in range(NT):
                    if n == CD0 + 12 and t == 1:
                        pe.wait_ge(probT_ready, 8)
                    f = slice(t * P, (t + 1) * P)
                    for a in range(2):
                        for h in range(2):
                            o = ps[:, 4 + 2 * t + h, :]
                            cs = slice(512 * h, 512 * h + 512)
                            pe.matmul(o, y_hi[:, a, f], hi[:, a, cs], start=(first and a == 0), stop=False)
                            pe.matmul(o, y_hi[:, a, f], lo[:, a, cs], start=False, stop=False)
                            ins = pe.matmul(o, y_lo[:, a, f], hi[:, a, cs], start=False, stop=(last and a == 1))
                    if last and t == 0:
                        ins.then_inc(y_ps, 1)
                ins.then_inc(tile_used, 1)

            def column(v, col, fill=False):
                for k in range(KD):
                    f = slice(k * P, (k + 1) * P)
                    ins = pe.matmul(ps[:, col[0], col[1] + k:col[1] + k + 1], acc_of[v][:, f], ones[:, 0:1], start=True, stop=True)
                    if k == KD - 1:
                        ins.then_inc(col_ps, 1)
                    if fill:
                        zeros(1)

            def gate_rows(v):
                for h in range(2):
                    cs = slice(512 * h, 512 * h + 512)
                    ins = pe.matmul(ps[:, 2 + h, :], ones[:, 0:1].to_broadcast([P, P]), acc_of[v][:, cs], start=True, stop=True)
                ins.then_inc(gate_ps, 1)

            def zeros(bank, count=1, stop=True):
                for _ in range(count):
                    pe.matmul(ps[:, bank, :], zero[:, :], zero[:, 0:1].to_broadcast([P, 512]), start=True, stop=stop)

            def transpose_x(m):
                if m:
                    zeros(1, WARM_X)
                for t in range(NT):
                    pe.wait_ge(xh_done, 2 * m + t + 1)
                    for b in range(4):
                        for a in range(2):
                            f = slice((2 * b + a) * P, (2 * b + a + 1) * P)
                            ins = pe.transpose(ps[:, b, a * TOK + t * P:a * TOK + (t + 1) * P], xh[:, t, f], ident[:, :])
                        if t == NT - 1:
                            ins.then_inc(xT_ps, 1)
                    if m:
                        pe.wait_ge(x_ready, 2 * m)
                        zeros(6, (WARM_T0, WARM_T1)[t])
                if m % 2:
                    for b in range(4, 8):
                        zeros(b, stop=False)

            pe.wait_ge(consts_ready, 1)
            pe.wait_ge(c_in, 16)
            pe.transpose(ps[:, 4, 0:KD], c_rows[:, :], ident[0:KD, 0:KD]).then_inc(cT_ps, 1)
            pe.wait_ge(rows_in, 16 * 5)
            pe.transpose(ps[:, 0, 0:R_ALL], small_rows[:, :], ident[0:R_ALL, 0:R_ALL])
            for t in range(3):
                ins = pe.transpose(ps[:, 1, 4 * FCH * t:4 * FCH * (t + 1)], conv_rows[:, t, :], ident[0:4 * FCH, 0:4 * FCH])
            ins.then_inc(rowsT_ps, 1)
            pe.wait_ge(small_ready, 2)
            transpose_x(0)
            pe.wait_ge(consts_ready, 3)
            pe.wait_ge(ada_step, 8)
            column(0, (5, 0))
            for done in range(10, 16):
                pe.wait_ge(ada_step, done)
                zeros(6, WARM_ADA)
            pe.wait_ge(ada_step, 16)
            column(1, (5, KD))
            pe.wait_ge(ws_masked, 1)
            for g in range(A_GROUPS):
                ins = pe.transpose(ps[:, 6 + g // 4, (g % 4) * P:(g % 4 + 1) * P], ws_raw[:, g, :], ident[:, :])
            ins.then_inc(wsT_ps, 1)
            zeros(4, WARM_H)

            def mix(j, bank):
                if j == 0:
                    pe.wait_ge(vn_ready, 1)
                for a in range(2):
                    g = 2 * j + a
                    for t in range(NT):
                        ins = pe.matmul(ps[:, bank, a * TOK + t * P:a * TOK + (t + 1) * P],
                                        vn[:, t, g * P:(g + 1) * P], wsT[:, g, :], start=True, stop=True)
                ins.then_inc(mix_ps, 1)

            pe.wait_ge(mod_ready, 1)
            for n in range(4):
                if n == 2:
                    pe.wait_ge(wsT_ready, 1)
                tile_M(n, 4 + 2 * (n // 2))
            tile_T(4, 0)
            tile_T(5, 1)
            tile_T(6, 2)
            pe.wait_ge(px_ready, 3)
            tile_T(7, 0)
            mix(0, 3)
            mix(1, 1)
            pe.wait_ge(gu_ready, 1)
            tile_T(8, 2)
            pe.wait_ge(pooled, NB)
            pe.wait_ge(ab_in, 16 * 4)
            for g in range(NB):
                s = (pool_a[:, 0, :], pool_b[:, 0, :], pool_a[:, 2, :], pool_b[:, 2, :])[g]
                ins = pe.matmul(ps[:, 6 + g // 2, (g % 2) * TOK:(g % 2 + 1) * TOK], pool_w[:, g, :],
                                s[:, PAD:PAD + TOK], start=True, stop=True)
            ins.then_inc(poolmix_ps, 1)
            pe.wait_ge(gu_ready, 2)
            tile_T(9, 0)
            pe.wait_ge(y_ready, 1)
            mix(2, 3)
            pe.wait_ge(y_ready, 2)
            mix(3, 1)
            pe.wait_ge(yb_f, 1)
            for n in range(10, FF0):
                pair = Y_PAIRS[n - 10]
                if pair[0] >= 8:
                    pe.wait_ge(yb_ready, 1)
                    y_hi, y_lo = yTb_hi[:, pair[0] - 8:pair[0] - 6, :], yTb_lo[:, pair[0] - 8:pair[0] - 6, :]
                else:
                    pe.wait_ge(y_ready, pair[0] // 2 + 1)
                    y_hi, y_lo = yTa_hi[:, pair[0]:pair[0] + 2, :], yTa_lo[:, pair[0]:pair[0] + 2, :]
                tile_Y(n, y_hi, y_lo, n == 10, n == FF0 - 1)
                if n == 12:
                    pe.wait_ge(ada_step, 2 * PRO + 8)
                    pe.wait_ge(y_ready, 3)
                    gate_rows(2)
                if n == 14:
                    pe.wait_ge(ada_step, 2 * PRO + 16)
                    pe.wait_ge(gu_ready, 4)
                    column(3, (0, 0))

            def ffn(l, base):
                first = 26 * l
                for h in range(2):
                    need(base + h)
                def accumulate(h, a, k):
                    f = slice(a * P, (a + 1) * P)
                    o = ps[:, h, a * TOK:(a + 1) * TOK]
                    hi, lo = as_k8(w_hi, (base + h) % RING), as_k8(w_lo, (base + h) % RING)
                    pe.matmul(o, hi[:, k, f], hT_hi[:, k, :], start=(k == 0), stop=False)
                    pe.matmul(o, hi[:, k, f], hT_lo[:, k, :], start=False, stop=False)
                    return pe.matmul(o, lo[:, k, f], hT_hi[:, k, :], start=False, stop=(k == KD - 1))

                for k in range(KD):
                    if k % 2 == 0:
                        pe.wait_ge(h_done, 8 * l + 4 + k // 2 + 1)
                    for h in range(2):
                        if k == 0:
                            pe.wait_ge(hf_done, 8 * l + 4 + h + 1)
                        accumulate(h, 0, k)
                for h in range(2):
                    for k in range(KD):
                        ins = accumulate(h, 1, k)
                    ins.then_inc(tile_used, 1)
                with pe.Fori(0, 5) as i:
                    for r in range(2):
                        q = 1 - r
                        for h in range(2):
                            pe.wait_ge(up_free, val(first + 2 * (1 + r) + h + 1, i, 4))
                            tile_T(base + 2 + 3 * r + h, 2 * q + h, i)
                        pe.wait_ge(aT_ready, val(13 * l + 3 + r, i, 2))
                        tile_Y(base + 4 + 3 * r, yTa_hi[:, 2 * r:2 * r + 2, :], yTa_lo[:, 2 * r:2 * r + 2, :], False, False, i)
                pe.wait_ge(ada_step, added(ADA_MID + TAIL0) if l == 0 else added(ADA_FF1) + LOOP_K)
                pe.wait_ge(up_free, first + 4 + 20)
                gate_rows(5 if l == 0 else 11)
                if l == 0:
                    pe.wait_ge(up_free, first + 4 + 22)
                    column(6, (0, 0))
                pe.wait_ge(aT_ready, 13 * l + 13)
                tile_Y(base + 32, yTa_hi[:, 0:2, :], yTa_lo[:, 0:2, :], False, True)

            pe.wait_ge(ada_step, 2 * PRO + 24)
            column(4, (0, KD), True)
            transpose_x(1)
            ffn(0, FF0)
            column(7, (0, KD), True)
            pe.wait_ge(mod_ready, 3)
            pe.wait_ge(gate_ready, 2)
            transpose_x(2)

            def transpose_qk(z):
                pe.wait_ge(rot_done, z + 1)
                for k in range(4):
                    for t in range(NT):
                        o = ps[:, 4 + 2 * z + k // 2, (k % 2) * TOK + t * P:(k % 2) * TOK + (t + 1) * P]
                        ins = pe.transpose(o, qk[:, z, t, k * P:(k + 1) * P], ident[:, :])
                ins.then_inc(qkT_ps, 1)

            def scores(h):
                if h >= 2:
                    pe.wait_ge(min_ready, h - 1)
                r = slice(HD * (h % 2), HD * (h % 2) + HD)
                b = 4 + h % 2
                pe.matmul(ps[:, b, 0:P], qT[r, h // 2, 0:P], kT[r, h // 2, 0:P], start=True, stop=True)
                pe.matmul(ps[:, b, P:3 * P], qT[r, h // 2, P:TOK], kT[r, h // 2, :], start=True, stop=True).then_inc(score_ps, 1)

            def transpose_p(h):
                pe.wait_ge(prob_ready, h + 1)
                if h >= 2:
                    pe.wait_ge(probT_ready, h - 1)
                for b in range(3):
                    ins = pe.transpose(ps[:, 6 + h % 2, b * P:(b + 1) * P], prob[:, h % 2, b * P:(b + 1) * P], ident[:, :])
                ins.then_inc(probT_ps, 1)

            def values(h):
                pe.wait_ge(probT_ready, h + 1)
                if h >= 2:
                    pe.wait_ge(yd_ready, h // 2)
                r = slice(HD * (h % 2), HD * (h % 2) + HD)
                c0 = TOK * (h // 2 % 2)
                pe.matmul(ps[r, 1, c0:c0 + TOK], vs[:, 0, h * HD:(h + 1) * HD], probT[:, h % 2, 0:TOK], start=True, stop=False)
                pe.matmul(ps[r, 1, c0 + P:c0 + TOK], vs[:, 1, h * HD:(h + 1) * HD], probT[:, h % 2, TOK:3 * P],
                          start=False, stop=True).then_inc(pv_ps, 1)

            for n in range(2):
                tile_M(CD0 + n, 4)
            for n in range(2, 4):
                tile_M(CD0 + n, 6)
            pe.wait_ge(hf_done, 12)
            for n in range(4, 6):
                tile_M(CD0 + n, 0)
            tile_T(CD0 + 6, 2)
            transpose_qk(0)
            transpose_qk(1)
            tile_T(CD0 + 7, 3)
            pe.wait_ge(qkT_ready, 2)
            scores(0)
            scores(1)
            pe.wait_ge(qkv_s, 3)
            tile_T(CD0 + 8, 0)
            for h in (0, 1):
                transpose_p(h)
            for h in (2, 3):
                scores(h)
            pe.wait_ge(ccs_ready, 1)
            tile_T(CD0 + 9, 2)
            for h in range(2):
                values(h)
                transpose_p(h + 2)
                scores(h + 4)
            pe.wait_ge(cm_ready, 1)
            tile_T(CD0 + 10, 3)
            for h in range(2, 4):
                values(h)
                transpose_p(h + 2)
                scores(h + 4)
            pe.wait_ge(yc_ready, 1)
            tile_T(CD0 + 11, 0)
            for h in range(4, 6):
                values(h)
                transpose_p(h + 2)
            for n in range(12, 16):
                j = n - 12
                if j < 2:
                    pe.wait_ge(yc_ready, j + 1)
                else:
                    pe.wait_ge(yd_ready, 2 * (j - 1))
                tile_Y(CD0 + n, yTa_hi[:, 2 * j:2 * j + 2, :], yTa_lo[:, 2 * j:2 * j + 2, :], n == 12, n == 15)
                if n == 12:
                    values(6)
                    values(7)
                    pe.wait_ge(ada_step, added(ADA_FF1 - LATE1))
                    gate_rows(8)
                if n == 13:
                    column(9, (0, 0))
            column(10, (0, KD), True)
            pe.wait_ge(mod_ready, 4)
            pe.wait_ge(gate_ready, 3)
            transpose_x(3)
            ffn(1, FF1)

        @block.vector
        def _(dve):
            st = Steps(dve, dve_step)
            a_next = [0]

            def split_lo(n, i=None):
                dve.wait_ge(hi_done, val(n + 1, i, 6))
                dve.tensor_tensor(w_lo[:, n % RING, 0:LO_DVE], raw[:, (n + PRO) % RAW, 0:LO_DVE],
                                  w_hi[:, n % RING, 0:LO_DVE].bitcast(F32), ALU.subtract).then_inc(lo_dve, 1)

            def ada_add(dst, src, k, before):
                if before is not None:
                    dve.wait_ge(ada_step, before)
                dve.scalar_tensor_tensor(dst, src, k, dst, ALU.mult, ALU.add).then_inc(ada_step, 1)

            def ada_tiles(count):
                for _ in range(count):
                    a = a_next[0]
                    v, k = ADA_TILES[a]
                    slot, before = ada_slot(a)
                    dve.wait_ge(ada_in[slot], 16 * (before + 1))
                    dve.wait_ge(bias_in[v], 16)
                    ada_add(acc_of[v], ada[:, slot, :], cact[:, k:k + 1], added(a))
                    a_next[0] += 1

            def split_both(src, hi, lo, signal):
                st.link(dve.tensor_copy(hi, src))
                dve.tensor_tensor(lo, src, hi.bitcast(F32), ALU.subtract).then_inc(signal, 1)

            def norm(m):
                for t in range(NT):
                    dve.wait_ge(rs_done, 4 * m + t + 1)
                    j = 4 * m + t
                    dve.tensor_scalar(xh[:, t, :], xs[:, t, :], rstd[:, j:j + 1], None, ALU.mult).then_inc(xh_done, 1)

            def split_h(m):
                for b in range(4):
                    dve.wait_ge(hf_done, 4 * m + b + 1)
                    split_both(h_room(b), hT_hi[:, 2 * b:2 * b + 2, :],
                               hT_lo[:, 2 * b:2 * b + 2, :], h_done)

            def shift_and_scale(m, col):
                g0 = R_NORM + 32 * (m // 2) + 16 * (m % 2)
                sh = ps[:, col[0], col[1]:col[1] + KD]
                sc = ps[:, col[0], col[1] + KD:col[1] + 2 * KD]
                dve.tensor_copy(mod[:, m, 0, :], sh)
                return dve.scalar_tensor_tensor(mod[:, m, 1, :], sc, 1.0, cols[:, g0:g0 + KD], ALU.add, ALU.mult)

            def gate_mul(r):
                dve.wait_ge(gate_ps, r + 1)
                dve.wait_ge(grow_in, 16 * (r + 1))
                dve.tensor_tensor(gate[:, :], ps[:, 2:4, :].rearrange("p b n -> p (b n)"), gate[:, :],
                                  ALU.mult).then_inc(gate_ready, 1)

            def residual(r):
                dve.wait_ge(gate_ready, r + 1)
                for t in range(NT):
                    j = 4 * r + t + 2
                    yg = xh[:, t, :]
                    dve.wait_ge(sq_done, 4 * r + t + 3)
                    st.link(dve.tensor_tensor(yg, y_of(t), gate[:, :], ALU.mult))
                    dve.wait_ge(rs_done, 4 * r + t + 3)
                    dve.scalar_tensor_tensor(xs[:, t, :], yg, rstd[:, j:j + 1], xs[:, t, :], ALU.mult, ALU.add).then_inc(x_ready, 1)

            def constants():
                dve.wait_ge(consts_ready, 3 + HALF + 1)
                st.link(dve.tensor_copy(cnt_f[:, :], cnt_i[:, :]))
                for g, w in enumerate(WINDOWS):
                    last = st.done(dve.tensor_scalar_min(inv_cnt[:, g, :], cnt_f[:, :], float(w)))
                st.wait(last)
                for g in range(NB):
                    st.done(dve.reciprocal(inv_cnt[:, g, :], inv_cnt[:, g, :]))
                dve.wait_ge(pos_in, 16)
                st.link(dve.tensor_copy(pos_f[:, :], pos_i[:, :]))
                for t in range(NT):
                    last = st.done(dve.tensor_scalar(angle[:, t * HALF:(t + 1) * HALF], inv_freq[:, :], pos_f[:, t:t + 1], None, ALU.mult))
                st.wait(last)
                two_pi = 2 * np.pi
                c1 = 6.28125
                c2 = float(np.float32(np.round((two_pi - c1) * 2 ** 21) / 2 ** 21))
                c3 = float(np.float32(two_pi - c1 - c2))
                for q in range(2):
                    last = st.done(dve.tensor_scalar(turns_i[:, q, :], angle[:, :], 1 / two_pi, 0.25 * q, ALU.mult, ALU.add))
                st.wait(last)
                kf = tmp[:, 0, 0:2 * NT * HALF].rearrange("p (q j) -> p q j", q=2)
                st.link(dve.tensor_copy(kf, turns_i[:, :, :]))
                for q in range(2):
                    last = st.done(dve.scalar_tensor_tensor(turns_f[:, q, :], kf[:, q, :], -c1, angle[:, :], ALU.mult, ALU.add))
                st.wait(last)
                for cc in (c2, c3):
                    st.link(dve.scalar_tensor_tensor(turns_f[:, :, :], kf, -cc, turns_f[:, :, :], ALU.mult, ALU.add))
                st.link(dve.tensor_scalar(turns_f[:, 1, :], turns_f[:, 1, :], float(np.pi / 2), None, ALU.add))
                pi_in = float(np.nextafter(np.float32(np.pi), np.float32(0)))
                dve.tensor_scalar(turns_f[:, :, :], turns_f[:, :, :], pi_in, -pi_in, ALU.min, ALU.max).then_inc(angles_ready, 1)

            for v in range(3):
                dve.memset(acc_of[v], 0.0).then_inc(acc_zero, 1)
            dve.wait_ge(cact_ready, 1)
            for m in range(PRO):
                dve.wait_ge(raw_in[m % RAW], 16 * (m // RAW + 1))
                for j in range(2):
                    k = 2 * (m % 4) + j
                    if k == 0:
                        dve.wait_ge(bias_in[m // 4], 16)
                    ada_add(acc_of[m // 4], raw[:, m % RAW, j * D:(j + 1) * D], cact[:, k:k + 1], 2 * m + j or None)
            dve.wait_ge(col_ps, 2)
            dve.wait_ge(small_ready, 1)
            shift_and_scale(0, (5, 0)).then_inc(mod_ready, 1)
            split_lo(0)
            split_h(0)

            split_lo(1)
            dve.wait_ge(wsT_ps, 1)
            dve.memset(pool_x[:, :, 0:PAD], 0.0).then_inc(px_ready, 1)
            constants()
            split_lo(2)

            def mixed(j):
                bank = (3, 1)[j % 2]
                dve.wait_ge(mix_ps, j + 1)
                if j:
                    dve.wait_ge(y_ready, j)
                b = bs[:, 2 * j:2 * j + 2, None, :].to_broadcast([P, 2, NT, P])
                st.link(dve.tensor_tensor(mx[:, :].rearrange("p (g t i) -> p g t i", g=2, t=NT),
                                          ps[:, bank, :].rearrange("p (g t i) -> p g t i", g=2, t=NT), b, ALU.add))
                dve.wait_ge(gu_ready, j + 1)
                st.link(dve.tensor_tensor(mx[:, :], mx[:, :], gu[:, j % 2, :], ALU.mult))
                if j == 0:
                    dve.wait_ge(poolmix_ps, 1)
                m = mx[:, :].rearrange("p (a t) -> p a t", a=2)
                split_both(m, yTa_hi[:, 2 * j:2 * j + 2, :], yTa_lo[:, 2 * j:2 * j + 2, :], y_ready)

            def window_means():
                W = PAD + TOK
                dve.wait_ge(window_sums, 1)
                sums_of = (pool_a[:, 0, :], pool_b[:, 0, :], pool_a[:, 2, :], pool_b[:, 2, :])
                for g in range(NB):
                    s = sums_of[g]
                    last = st.done(dve.tensor_tensor(s[:, PAD:2 * PAD], s[:, PAD:2 * PAD], inv_cnt[:, g, :], ALU.mult))
                st.wait(last)
                for g, w in enumerate(WINDOWS):
                    s = sums_of[g]
                    st.done(dve.tensor_tensor(s[:, PAD:2 * PAD], s[:, PAD:2 * PAD], pool_x[:, g, PAD:2 * PAD], ALU.subtract))
                    dve.scalar_tensor_tensor(s[:, 2 * PAD:W], s[:, 2 * PAD:W], 1.0 / w, pool_x[:, g, 2 * PAD:W],
                                             ALU.mult, ALU.subtract).then_inc(pooled, 1)

            for n in range(AB0, FF0):
                if n in (1, 3):
                    h = n // 2
                    dve.wait_ge(v_ready, h + 1)
                    for t in range(NT):
                        last = st.done(dve.bn_stats(v_stat[:, t, h, :], vn[:, t, 512 * h:512 * h + 512]))
                if n == 3:
                    st.wait(last)
                    st.done(dve.bn_aggr(v_mv[:, 0, :], v_stat[:, 0, :, :]))
                    dve.bn_aggr(v_mv[:, 1, :], v_stat[:, 1, :, :]).then_inc(v_var, 1)
                    dve.wait_ge(ab_in, 16 * 4)
                    for t in range(NT):
                        dve.wait_ge(v_rstd, t + 1)
                        last = st.done(dve.tensor_scalar(vn[:, t, :], vn[:, t, :], v_mv[:, t, 0:1], rstd[:, 16 + t:17 + t],
                                                         ALU.subtract, ALU.mult))
                if n == 9:
                    mixed(2)
                    mixed(3)
                if n == 10:
                    dve.wait_ge(yb_f, 1)
                    split_both(tmp[:, :, :], yTb_hi[:, :, :], yTb_lo[:, :, :], yb_ready)
                if n == 13:
                    gate_mul(0)
                if n < FF0 - 1:
                    split_lo(n + RING)
                    if n == 3:
                        st.wait(last)
                        st.link(dve.tensor_tensor(vn[:, :, :], vn[:, :, :], vg[:, None, :].to_broadcast([P, NT, D]), ALU.mult))
                        dve.tensor_tensor(vn[:, :, :], vn[:, :, :], vb[:, None, :].to_broadcast([P, NT, D]), ALU.add).then_inc(vn_ready, 1)
                    if n == 6:
                        window_means()
                    if n == 7:
                        mixed(0)
                        mixed(1)
                    ada_tiles(ADA_AB.get(n + RING, 0))

            def ffn(l, base):
                def conv(k, i, par):
                    for h in range(2):
                        dve.wait_ge(tap_done, val(22 * l + 2 * k + h + 1, i, 4))
                        for back in (1, 2):
                            for a in range(2):
                                col = 2 * FCH * l + FCH * h + 2 * k + a
                                o = cbuf[:, par, h, a * TOK + back:(a + 1) * TOK]
                                ins = dve.scalar_tensor_tensor(
                                    o, ps[:, 2 * par + h, a * TOK:(a + 1) * TOK - back],
                                    ffn_cols[:, 2 - back, bass.ds(val(col, i, 4), 1)], o, ALU.mult, ALU.add)
                                if back == 1 or a == 0:
                                    last = st.done(ins)
                            if back == 1:
                                st.wait(last)
                        ins.then_inc(up_free, 1)

                def gated(k, i, par):
                    dve.wait_ge(silu_done, val(11 * l + k + 1, i, 2))
                    dve.wait_ge(up_free, val(26 * l + 4 + 2 * k + 2, i, 4))
                    dve.wait_ge(tile_used, val(base + 3 * k - 1, i, 6))
                    st.link(dve.tensor_tensor(cbuf[:, par, 1, :], cbuf[:, par, 0, :], cbuf[:, par, 1, :], ALU.mult))
                    s = cbuf[:, par, 1, :].rearrange("p (a t) -> p a t", a=2)
                    st.link(dve.tensor_copy(yTa_hi[:, 2 * par:2 * par + 2, :], s))
                    dve.tensor_tensor(yTa_lo[:, 2 * par:2 * par + 2, :], s,
                                      yTa_hi[:, 2 * par:2 * par + 2, :].bitcast(F32), ALU.subtract).then_inc(aT_ready, 1)

                def loop_ada(i, r, j):
                    k = cact[:, bass.ds(i, 1)]
                    before = ADA_FF // 3
                    if l == 0 and j < 2:
                        dve.wait_ge(ada_in[j], val(16 * (before + r + 1), i, 32))
                        ada_add(acc_of[LOOP_V[2 * r + j]], ada[:, j, :], k, val(added(ADA_FF) + 3 * r + j, i, LOOP_ADDS))
                    elif l == 0 and r == 0:
                        dve.wait_ge(ada_in[2], val(16 * (before + 1), i, 16))
                        ada_add(acc_of[5], ada[:, 2, :], k, val(added(ADA_FF) + 2, i, LOOP_ADDS))
                    elif l == 1 and r == 0 and j == 0:
                        before = sum(ada_slot(a)[0] == 2 for a in (*range(ADA_FF), *range(ADA_MID, ADA_FF1))) + LOOP_K
                        dve.wait_ge(ada_in[2], val(16 * (before + 1), i, 16))
                        ada_add(acc_of[11], ada[:, 2, :], k, val(added(ADA_FF1), i, 1))

                dve.sem_inc(up_free, 4)
                dve.sem_inc(aT_ready, 2)
                split_lo(base + 2)
                ada_tiles((LATE0, LATE1)[l])
                if l == 0:
                    for v in (5, 9, 10):
                        dve.wait_ge(bias_in[v], 16)
                with dve.Fori(0, 5) as i:
                    st.enter(i, 2 * 8)
                    for r in range(2):
                        split_lo(base + 3 + 3 * r, i)
                        conv(r, i, r)
                        loop_ada(i, r, 0)
                        gated(r, i, r)
                        split_lo(base + 4 + 3 * r, i)
                        loop_ada(i, r, 1)
                        split_lo(base + 5 + 3 * r, i)
                        loop_ada(i, r, 2)
                    st.leave(5)
                if l == 0:
                    a_next[0] = ADA_MID
                    ada_tiles(TAIL0)
                conv(10, None, 0)
                gated(10, None, 0)
                gate_mul(2 * l + 1)
                if l == 0:
                    split_lo(base + 33)
                    split_lo(base + 34)

            residual(0)
            dve.wait_ge(col_ps, 4)
            shift_and_scale(1, (0, 0)).then_inc(mod_ready, 1)
            norm(1)
            split_h(1)
            ffn(0, FF0)
            residual(1)
            dve.wait_ge(col_ps, 6)
            shift_and_scale(2, (0, 0)).then_inc(mod_ready, 1)
            norm(2)
            split_h(2)
            split_lo(CD0 + 2)

            def rotate(z):
                dve.wait_ge(qkv_s, z + 1)
                if z == 0:
                    dve.wait_ge(trig_ready, 1)
                else:
                    dve.wait_ge(rot_done, 1)
                v = qk[:, z, :, :].rearrange("p t (h d) -> p t h d", h=HEADS)
                x1, x2 = v[:, :, :, 0:HALF], v[:, :, :, HALF:ROT]
                sin = trig[:, 0, :, None, :].to_broadcast([P, NT, HEADS, HALF])
                cos = trig[:, 1, :, None, :].to_broadcast([P, NT, HEADS, HALF])
                t = [tmp[:, j, 0:P].rearrange("p (t h d) -> p t h d", t=NT, h=HEADS) for j in range(4)]
                for o, u, w in ((t[0], x1, cos), (t[1], x2, sin), (t[2], x2, cos), (t[3], x1, sin)):
                    last = st.done(dve.tensor_tensor(o, u, w, ALU.mult))
                st.wait(last)
                st.done(dve.tensor_tensor(x1, t[0], t[1], ALU.subtract))
                dve.tensor_tensor(x2, t[2], t[3], ALU.add).then_inc(rot_done, 1)

            def lowest(h):
                dve.wait_ge(score_ps, h + 1)
                if h == 0:
                    dve.wait_ge(mask_ready, 2)
                if h >= 2:
                    dve.wait_ge(probT_ps, h - 1)
                st.link(dve.scalar_tensor_tensor(prob[:, h % 2, :], ps[:, 4 + h % 2, 0:3 * P], -float(HD) ** -0.5, mask[:, :],
                                                 ALU.mult, ALU.add))
                for q in range(NT):
                    ins = dve.tensor_reduce(s_min[:, h % 2, q:q + 1], prob[:, h % 2, (0, P)[q]:(P, 3 * P)[q]], AX_X, ALU.min)
                    if q == 0:
                        st.done(ins)
                ins.then_inc(min_ready, 1)

            def normalise(h):
                dve.wait_ge(exp_done, h + 1)
                st.link(dve.reciprocal(s_sum[:, h % 2, :], s_sum[:, h % 2, :]))
                for q in range(NT):
                    s = prob[:, h % 2, (0, P)[q]:(P, 3 * P)[q]]
                    ins = dve.tensor_scalar(s, s, s_sum[:, h % 2, q:q + 1], None, ALU.mult)
                    if q == 0:
                        st.done(ins)
                ins.then_inc(prob_ready, 1)

            def softmax(h):
                lowest(h)
                lowest(h + 1)
                normalise(h)
                normalise(h + 1)

            def heads_out(j):
                dve.wait_ge(pv_ps, 2 * j + 2)
                split_both(ps[:, 1, TOK * (j % 2):TOK * (j % 2) + TOK], yTa_hi[:, 4 + j, :], yTa_lo[:, 4 + j, :], yd_ready)

            def gated_input(j):
                dve.wait_ge(ccs_ready, j + 1)
                dve.wait_ge(tile_used, CD0 + 8 + 3 * j)
                if j:
                    dve.wait_ge(yc_ready, j)
                dve.tensor_tensor(cm[:, :, :].rearrange("p a t -> p (a t)"), ccs[:, :, :].rearrange("p a t -> p (a t)"),
                                  ps[:, 3, :], ALU.mult).then_inc(cm_ready, 1)

            def gated_conv(j):
                dve.wait_ge(ctap_done, j + 1)
                for back in (1, 2):
                    for a in range(2):
                        col = R_CONV + 4 * (2 - back) + 2 * j + a
                        last = st.done(dve.scalar_tensor_tensor(cy[:, a, back:TOK], cm[:, a, 0:TOK - back], cols[:, col:col + 1],
                                                                cy[:, a, back:TOK], ALU.mult, ALU.add))
                    st.wait(last)
                dve.wait_ge(tile_used, CD0 + 9 + 3 * j)
                f = cy[:, :, :].rearrange("p a t -> p (a t)")
                st.link(dve.tensor_tensor(f, f, ps[:, 0, :], ALU.mult))
                split_both(cy[:, :, :], yTa_hi[:, 2 * j:2 * j + 2, :], yTa_lo[:, 2 * j:2 * j + 2, :], yc_ready)

            for n in range(16):
                if n == 14:
                    gate_mul(2)
                if n < 15:
                    split_lo(CD0 + n + RING)
                    ada_tiles(ADA_CD.get(CD0 + n + RING, 0))
                if n in (1, 3):
                    rotate(n // 2)
                if n == 7:
                    gated_input(0)
                    softmax(0)
                if n == 8:
                    gated_conv(0)
                    softmax(2)
                if n == 9:
                    heads_out(0)
                    softmax(4)
                if n == 10:
                    gated_input(1)
                    heads_out(1)
                    softmax(6)
                if n == 11:
                    gated_conv(1)
                    heads_out(2)
                if n == 12:
                    heads_out(3)
            residual(2)
            dve.wait_ge(col_ps, 8)
            shift_and_scale(3, (0, 0)).then_inc(mod_ready, 1)
            norm(3)
            split_h(3)
            ffn(1, FF1)
            residual(3)


_INS = ["x", "c", "positions", "ab_w_in", "ab_vnorm_g", "ab_vnorm_b", "ab_spatial_w", "ab_spatial_b", "ab_pool_w",
        "ab_pool_scale", "ab_w_out", "cd_w_in", "cd_conv_w", "cd_w_out", "ffn_w_up", "ffn_conv_w", "ffn_w_down",
        "ada_w", "ada_b", "norm_g"]


def kernel(**inputs):
    import concourse.bacc as bacc
    from concourse.bass_utils import run_bass_kernel_spmd

    nc = bacc.Bacc("TRN2", target_bir_lowering=False, num_devices=1)
    arrays, args = {}, []
    for name in _INS:
        a = np.ascontiguousarray(inputs[name])
        arrays[f"in_{name}"] = a
        args.append(nc.dram_tensor(f"in_{name}", a.shape, mybir.dt.from_np(a.dtype), kind="ExternalInput").ap())
    out = nc.dram_tensor("out", (1, TOK, D), F32, kind="ExternalOutput").ap()
    trunk(nc, *args, out)
    r = run_bass_kernel_spmd(nc, [arrays], core_ids=[0])
    return r.results[0]["out"]
```
